# Optimizing a Trainium2 kernel written in Bass

```python
import math
import jax, jax.numpy as jnp
from jax import lax
import numpy as np

D_MODEL = 1024
BATCH = 1
SEQ = 512
DEPTH = 2

N_MIXERS = 2
N_ATTN_LAYERS = (DEPTH + 1) // 2
N_DELTA_LAYERS = DEPTH // 2
PLE_DIM = 256
EPS = 1e-6

SWA_GROUPS = ((128, 1), (512, 4), (2048, 16))
N_GROUPS = len(SWA_GROUPS)
A_HEADS = 8
A_HEAD_DIM = 64
A_OUT_WIDTH = A_HEADS * A_HEAD_DIM
A_QKV_WIDTH = N_GROUPS * 3 * A_OUT_WIDTH
ROPE_DIM = A_HEAD_DIM // 4
ROPE_THETA = 500000.0
BAND_BLOCK = 128

DN_HEADS = 8
DN_HEAD_DIM = 128
DN_WIDTH = DN_HEADS * DN_HEAD_DIM
DN_IN_WIDTH = 3 * DN_WIDTH + 2 * DN_HEADS + DN_WIDTH
CONV_WIDTH = 4
CHUNK = 64

D_FF = 4 * D_MODEL

kernel_name = 'hybrid_dilated_swa_gated_deltanet'

def rmsnorm(x, gain):
    xf = x.astype(jnp.float32)
    y = xf * lax.rsqrt(jnp.mean(xf * xf, axis=-1, keepdims=True) + EPS)
    return (y * gain.astype(jnp.float32)).astype(x.dtype)

def l2norm(x):
    xf = x.astype(jnp.float32)
    return xf * lax.rsqrt(jnp.sum(xf * xf, axis=-1, keepdims=True) + EPS)

def rope_tables(positions):
    inv_freq = ROPE_THETA ** (-jnp.arange(0, ROPE_DIM, 2, dtype=jnp.float32) / ROPE_DIM)
    ang = positions.astype(jnp.float32)[..., None] * inv_freq
    return jnp.cos(ang)[:, :, None, :], jnp.sin(ang)[:, :, None, :]

def apply_partial_rope(x, cos, sin):
    half = ROPE_DIM // 2
    xf = x.astype(jnp.float32)
    x1, x2 = xf[..., :half], xf[..., half:ROPE_DIM]
    out = jnp.concatenate([x1 * cos - x2 * sin, x2 * cos + x1 * sin, xf[..., ROPE_DIM:]], axis=-1)
    return out.astype(x.dtype)

def dilated_band_attention(q, k, v, window, dilation):
    B, S, H, E = q.shape
    L = S // dilation
    span = window // dilation
    n_prev = -(-span // BAND_BLOCK)
    nblk = -(-L // BAND_BLOCK)
    Lp = nblk * BAND_BLOCK

    def by_residue(t):
        t = t.reshape(B, L, dilation, H, E).transpose(0, 2, 1, 3, 4)
        t = jnp.pad(t, ((0, 0), (0, 0), (0, Lp - L), (0, 0), (0, 0)))
        return t.reshape(B, dilation, nblk, BAND_BLOCK, H, E)

    def band(t):
        tp = jnp.pad(t, ((0, 0), (0, 0), (n_prev, 0), (0, 0), (0, 0), (0, 0)))
        return jnp.concatenate([tp[:, :, s:s + nblk] for s in range(n_prev + 1)], axis=3)

    qb = by_residue(q)
    kw = band(by_residue(k))
    vw = band(by_residue(v))
    qi = jnp.arange(BAND_BLOCK)[:, None]
    kj = jnp.arange((n_prev + 1) * BAND_BLOCK)[None, :]
    dist = qi + n_prev * BAND_BLOCK - kj
    k_abs = (jnp.arange(nblk)[:, None, None] - n_prev) * BAND_BLOCK + kj[None]
    valid = (dist >= 0)[None] & (dist <= span)[None] & (k_abs >= 0)

    s = jnp.einsum('bdnqhe,bdnkhe->bdnhqk', qb, kw).astype(jnp.float32) * (E ** -0.5)
    s = jnp.where(valid[None, None, :, None], s, -jnp.inf)
    m = jnp.max(s, axis=-1, keepdims=True)
    e = jnp.exp(s - m)
    l = jnp.sum(e, axis=-1, keepdims=True)
    o = jnp.einsum('bdnhqk,bdnkhe->bdnqhe', (e / l).astype(v.dtype), vw)
    lse = (m + jnp.log(l))[..., 0]
    o = o.reshape(B, dilation, Lp, H, E)[:, :, :L].transpose(0, 2, 1, 3, 4).reshape(B, S, H, E)
    lse = lse.transpose(0, 1, 2, 4, 3).reshape(B, dilation, Lp, H)[:, :, :L]
    lse = lse.transpose(0, 2, 1, 3).reshape(B, S, H)
    return o, lse

def dilated_attention_mixer(h, cos, sin, w_qkv, q_gain, k_gain, w_o):
    B, S, _ = h.shape
    qkv = (h @ w_qkv).reshape(B, S, N_GROUPS, 3, A_HEADS, A_HEAD_DIM)
    outs, lses = [], []
    for g, (window, dilation) in enumerate(SWA_GROUPS):
        q = apply_partial_rope(rmsnorm(qkv[:, :, g, 0], q_gain[g]), cos, sin)
        k = apply_partial_rope(rmsnorm(qkv[:, :, g, 1], k_gain[g]), cos, sin)
        o, lse = dilated_band_attention(q, k, qkv[:, :, g, 2], window, dilation)
        outs.append(o)
        lses.append(lse)
    wts = jax.nn.softmax(jnp.stack(lses, axis=0), axis=0)
    o = jnp.einsum('gbsh,gbshe->bshe', wts.astype(h.dtype), jnp.stack(outs, axis=0))
    return o.reshape(B, S, A_OUT_WIDTH) @ w_o

def causal_depthwise_conv(x, w):
    C = x.shape[-1]
    return lax.conv_general_dilated(
        x, w[:, None, :].astype(x.dtype), window_strides=(1,),
        padding=[(CONV_WIDTH - 1, 0)], dimension_numbers=('NWC', 'WIO', 'NWC'),
        feature_group_count=C)

def to_chunks(t):
    B, S = t.shape[:2]
    t = t.reshape(B, S // CHUNK, CHUNK, *t.shape[2:])
    return jnp.moveaxis(t, 2, 3)

def chunk_gated_delta_rule(q, k, v, g, beta):
    B, S, H, K = q.shape
    V = v.shape[-1]
    qc, kc, vc = to_chunks(q), to_chunks(k), to_chunks(v)
    gc = jnp.cumsum(to_chunks(g), axis=-1)
    bc = to_chunks(beta)[..., None]
    lower = jnp.tril(jnp.ones((CHUNK, CHUNK), dtype=bool))
    strict = jnp.tril(jnp.ones((CHUNK, CHUNK), dtype=bool), -1)
    decay = jnp.exp(jnp.where(lower, gc[..., :, None] - gc[..., None, :], -jnp.inf))
    kb = kc * bc
    a_mat = jnp.where(strict, jnp.einsum('bnhik,bnhjk->bnhij', kb, kc) * decay, 0.0)
    rhs = jnp.concatenate([vc * bc, kb * jnp.exp(gc)[..., None]], axis=-1)
    sol = lax.linalg.triangular_solve(a_mat + jnp.eye(CHUNK, dtype=a_mat.dtype), rhs,
                                      left_side=True, lower=True, unit_diagonal=True)
    u, w = sol[..., :V], sol[..., V:]
    attn = jnp.einsum('bnhik,bnhjk->bnhij', qc, kc) * decay
    q_dec = qc * jnp.exp(gc)[..., None]
    k_dec = kc * jnp.exp(gc[..., -1:] - gc)[..., None]
    c_dec = jnp.exp(gc[..., -1])

    def step(state, inp):
        u_i, w_i, qd_i, kd_i, at_i, cd_i = inp
        v_new = u_i - jnp.einsum('bhck,bhkv->bhcv', w_i, state)
        o_i = jnp.einsum('bhck,bhkv->bhcv', qd_i, state) + jnp.einsum('bhij,bhjv->bhiv', at_i, v_new)
        state = state * cd_i[..., None, None] + jnp.einsum('bhck,bhcv->bhkv', kd_i, v_new)
        return state, o_i

    xs = tuple(jnp.moveaxis(t, 1, 0) for t in (u, w, q_dec, k_dec, attn, c_dec))
    state0 = jnp.zeros((B, H, K, V), dtype=jnp.float32)
    _, o = lax.scan(step, state0, xs)
    return jnp.moveaxis(o, 0, 1).swapaxes(2, 3).reshape(B, S, H, V)

def gated_deltanet_mixer(h, w_in, conv_w, a_log, dt_bias, o_gain, w_o):
    B, S, _ = h.shape
    proj = h @ w_in
    c = 3 * DN_WIDTH
    qkv = proj[..., :c]
    a = proj[..., c:c + DN_HEADS]
    b = proj[..., c + DN_HEADS:c + 2 * DN_HEADS]
    z = proj[..., c + 2 * DN_HEADS:]
    qkv = jax.nn.silu(causal_depthwise_conv(qkv, conv_w))
    q, k, v = jnp.split(qkv, 3, axis=-1)
    q = l2norm(q.reshape(B, S, DN_HEADS, DN_HEAD_DIM)) * (DN_HEAD_DIM ** -0.5)
    k = l2norm(k.reshape(B, S, DN_HEADS, DN_HEAD_DIM))
    v = v.reshape(B, S, DN_HEADS, DN_HEAD_DIM).astype(jnp.float32)
    beta = jax.nn.sigmoid(b.astype(jnp.float32))
    g = -jnp.exp(a_log.astype(jnp.float32)) * jax.nn.softplus(a.astype(jnp.float32) + dt_bias.astype(jnp.float32))
    o = chunk_gated_delta_rule(q, k, v, g, beta)
    o = rmsnorm(o, o_gain) * jax.nn.silu(z.reshape(B, S, DN_HEADS, DN_HEAD_DIM).astype(jnp.float32))
    return o.reshape(B, S, DN_WIDTH).astype(h.dtype) @ w_o

def setup_inputs(seed: int = 0) -> dict:
    key = jax.random.key(seed)
    ks = jax.random.split(key, 20)
    NA, NB = N_ATTN_LAYERS, N_DELTA_LAYERS

    def nrm(k, shape, fan_in):
        return jax.random.normal(k, shape, jnp.float32) * (fan_in ** -0.5)

    def gain(k, shape):
        return 1.0 + 0.02 * jax.random.normal(k, shape, jnp.float32)

    dt = jnp.exp(jax.random.uniform(ks[9], (NB, DN_HEADS), jnp.float32,
                                    minval=math.log(1e-3), maxval=math.log(1e-1)))
    return {
        'x': jax.random.normal(ks[0], (BATCH, SEQ, D_MODEL), jnp.float32),
        'p': jax.random.normal(ks[1], (DEPTH, BATCH, SEQ, PLE_DIM), jnp.float32),
        'positions': jnp.broadcast_to(jnp.arange(SEQ, dtype=jnp.int32), (BATCH, SEQ)),
        'mix_norm': gain(ks[2], (DEPTH, D_MODEL)),
        'attn_w_qkv': nrm(ks[3], (NA, D_MODEL, A_QKV_WIDTH), D_MODEL),
        'attn_q_gain': gain(ks[4], (NA, N_GROUPS, A_HEAD_DIM)),
        'attn_k_gain': gain(ks[5], (NA, N_GROUPS, A_HEAD_DIM)),
        'attn_w_o': nrm(ks[6], (NA, A_OUT_WIDTH, D_MODEL), A_OUT_WIDTH),
        'dn_w_in': nrm(ks[7], (NB, D_MODEL, DN_IN_WIDTH), D_MODEL),
        'dn_conv': nrm(ks[8], (NB, CONV_WIDTH, 3 * DN_WIDTH), CONV_WIDTH),
        'dn_a_log': jnp.log(jax.random.uniform(ks[10], (NB, DN_HEADS), jnp.float32, minval=1.0, maxval=16.0)),
        'dn_dt_bias': dt + jnp.log(-jnp.expm1(-dt)),
        'dn_o_gain': gain(ks[11], (NB, DN_HEAD_DIM)),
        'dn_w_o': nrm(ks[12], (NB, DN_WIDTH, D_MODEL), DN_WIDTH),
        'mlp_norm': gain(ks[13], (DEPTH, D_MODEL)),
        'w_up': nrm(ks[14], (DEPTH, D_MODEL, D_FF), D_MODEL),
        'w_down': nrm(ks[15], (DEPTH, D_FF, D_MODEL), D_FF),
        'ple_norm': gain(ks[16], (DEPTH, D_MODEL)),
        'w_ple': nrm(ks[17], (DEPTH, PLE_DIM, D_MODEL), PLE_DIM),
        'w_ple_gate': nrm(ks[18], (DEPTH, D_MODEL, D_MODEL), D_MODEL),
    }

def reference(x, p, positions, mix_norm, attn_w_qkv, attn_q_gain, attn_k_gain, attn_w_o,
              dn_w_in, dn_conv, dn_a_log, dn_dt_bias, dn_o_gain, dn_w_o,
              mlp_norm, w_up, w_down, ple_norm, w_ple, w_ple_gate):
    cos, sin = rope_tables(positions)
    for i in range(DEPTH):
        j = i // N_MIXERS
        hn = rmsnorm(x, mix_norm[i])
        if i % N_MIXERS == 0:
            mix = dilated_attention_mixer(hn, cos, sin, attn_w_qkv[j], attn_q_gain[j],
                                          attn_k_gain[j], attn_w_o[j])
        else:
            mix = gated_deltanet_mixer(hn, dn_w_in[j], dn_conv[j], dn_a_log[j], dn_dt_bias[j],
                                       dn_o_gain[j], dn_w_o[j])
        x = x + mix
        hn = rmsnorm(x, mlp_norm[i])
        x = x + jnp.square(jax.nn.relu(hn @ w_up[i])) @ w_down[i]
        gate = jax.nn.sigmoid((rmsnorm(x, ple_norm[i]) @ w_ple_gate[i]).astype(jnp.float32)).astype(x.dtype)
        x = x + (p[i] @ w_ple[i]) * gate
    return x


_drawn_inputs = setup_inputs


def setup_inputs(seed=0):
    import zlib

    import numpy as np

    out = dict(_drawn_inputs(seed))
    spreads = {}
    factors = {'mix_norm': 4.229,
     'attn_q_gain': 8.0,
     'attn_k_gain': 8.0,
     'dn_o_gain': 21.716,
     'ple_norm': 64.0,
     'mlp_norm': 5.322}
    for name, (base, spread) in spreads.items():
        noise = np.random.default_rng([zlib.crc32(name.encode()), seed]).standard_normal(out[name].shape)
        drawn = base * np.exp(spread * noise) if base else spread * noise
        out[name] = __import__('jax').numpy.asarray(drawn.astype(out[name].dtype))
    for name, factor in factors.items():
        out[name] = (out[name] * factor).astype(out[name].dtype)
    return out
```

```python
from contextlib import ExitStack

import numpy as np
import concourse.bass as bass
from concourse import mybir

F32 = mybir.dt.float32
F32R = mybir.dt.float32r
I32 = mybir.dt.int32
ALU = mybir.AluOpType
ACT = mybir.ActivationFunctionType
AX = mybir.AxisListType.X

P = 128
S = 512
D = 1024
KT = D // P
TT = S // P
FF = 4 * D
CH = 2048
EPS = 1e-6

HD = 64
AH = 8
AW = AH * HD
GROUPS = ((2, 4), (1, 4), (0, 1))
REC = AW + 2 * AH
ASCALE = HD ** -0.5
NEG = -1e30
RD = 16
HR = RD // 2

NH = 8
QS = float(P) ** -0.5
LEVELS = 7

C_AO, C_MLP, C_GATE, C_DN, C_DO = 18, (20, 77), (53, 110), 57, 73
N_CHUNKS = 114
T_AO, T_MLP, T_GATE, T_DO = 72, (80, 168), (152, 240), 160
NB = 4


_C = {}
_at = 0
for _n, _w in (("ident", P), ("incl", P), ("ones", P), ("strict", P), ("band", 2 * P), ("resid", P),
               ("lev", LEVELS * 64), ("freq", HR), ("eps", 1)):
    _C[_n] = (_at, _at + _w)
    _at += _w
N_CONST = _at
_P = {}
_at = 0
for _n, _w in (("gain", 6 * KT), ("qg", 3 * HD), ("kg", 3 * HD), ("conv", NH * 12), ("og", 1),
               ("dt", NH), ("alog", NH)):
    _P[_n] = (_at, _at + _w)
    _at += _w
N_PARAM = _at


def constants():
    i = np.arange(P)
    c = np.zeros((P, N_CONST), np.float32)

    def put(name, v):
        c[:, _C[name][0]:_C[name][1]] = v

    put("ident", np.eye(P))
    put("incl", i[:, None] <= i[None, :])
    put("ones", 1.0)
    put("strict", i[:, None] < i[None, :])
    put("band", np.concatenate([np.where(i[None, :] >= i[:, None], 0.0, NEG),
                                np.where(i[None, :] <= i[:, None], 0.0, NEG)], axis=1))
    same = (i[:, None] % 4) == (i[None, :] % 4)
    put("resid", np.where(same & (i[None, :] <= i[:, None]), 0.0, NEG))
    lev = []
    for n in range(LEVELS):
        b = 1 << n
        even = i[(i // b) % 2 == 0]
        lev.append(((i[:, None] // b) % 2 == 1) & ((i[:, None] // (2 * b)) == (even[None, :] // (2 * b))))
    put("lev", np.concatenate(lev, axis=1))
    put("freq", 500000.0 ** (-np.arange(0, RD, 2) / RD))
    put("eps", EPS)
    return c


class Chain:

    def __init__(self, eng, sem, base=0):
        self.eng, self.sem, self.base, self.n = eng, sem, base, 0

    def __call__(self, ins):
        self.n += 1
        ins.then_inc(self.sem, 1)
        self.eng.wait_ge(self.sem, self.base + self.n)


def rsqrt(dve, link, x, y, t, done=None):
    link(dve.tensor_scalar(t.bitcast(I32), x.bitcast(I32), 1, None, ALU.logical_shift_right))
    link(dve.tensor_scalar(y.bitcast(I32), t.bitcast(I32), -1.0, float(0x5F3759DF), ALU.mult, ALU.add))
    for step in range(3):
        link(dve.tensor_tensor(t, y, y, ALU.mult))
        link(dve.scalar_tensor_tensor(t, t, -0.5, x, ALU.mult, ALU.mult))
        last = dve.scalar_tensor_tensor(y, t, 1.5, y, ALU.add, ALU.mult)
        if step == 2 and done is not None:
            last.then_inc(done, 1)
        else:
            link(last)


def wait(eng, sem, count):
    if not isinstance(count, int) or count > 0:
        eng.wait_ge(sem, count)




def trunk(nc, xT, pT, pos, weights, wab, consts, params, scratch, out):
    ctx = ExitStack()
    with ctx:
        def sb(name, shape, dt=F32):
            return ctx.enter_context(nc.sbuf_tensor(name, [P] + shape, dt))

        def sem(name):
            return ctx.enter_context(nc.semaphore(name))

        x = sb("x_res", [KT, S])
        A_hi, A_lo = sb("A_hi", [KT, S], F32R), sb("A_lo", [KT, S], F32R)
        B_hi, B_lo = sb("B_hi", [KT, S], F32R), sb("B_lo", [KT, S], F32R)
        raw = sb("raw", [2, CH])
        w_hi, w_lo = sb("w_hi", [2, CH], F32R), sb("w_lo", [2, CH], F32R)
        cst, par = sb("cst", [N_CONST]), sb("par", [N_PARAM])
        work, small = sb("work", [17100]), sb("small", [1000])
        posi, kint = sb("posi", [8], I32), sb("kint", [8 * HR], I32)
        ab_hi, ab_lo = sb("ab_hi", [KT, 16], F32R), sb("ab_lo", [KT, 16], F32R)
        pg = [ctx.enter_context(nc.psum_tensor(f"pg{i}", [P, 512], F32)) for i in range(NB)]
        pa = [ctx.enter_context(nc.psum_tensor(f"pa{i}", [P, 512], F32)) for i in range(4)]

        used = {}

        def carve(pool, n, at=None):
            t = work if pool == "work" else small
            a = used.get(pool, 0) if at is None else at
            used[pool] = a + n
            assert used[pool] <= t.shape[1], (pool, used[pool])
            return t[:, a:a + n]

        def C(name, a=0, b=None):
            lo, hi = _C[name]
            return cst[:, lo + a:(hi if b is None else lo + b)]

        def Pm(name, a=0, b=None):
            lo, hi = _P[name]
            return par[:, lo + a:(hi if b is None else lo + b)]

        ident, ones = C("ident"), C("ones")

        rstd = carve("work", S)
        sq = [carve("work", S) for _ in range(2)]
        acc = carve("work", S)
        sdev = carve("work", S)
        relu = [carve("work", S) for _ in range(2)]
        act2 = [carve("work", S) for _ in range(2)]
        ple = carve("work", KT * S).rearrange("p (k s) -> p k s", k=KT)
        p_raw = carve("work", 2 * S)
        y_k, y_q = carve("work", TT * REC, 0), carve("work", TT * REC)
        qT = carve("work", TT * AW).rearrange("p (a s) -> p a s", a=4)
        kT = carve("work", TT * AW).rearrange("p (a s) -> p a s", a=4)
        V = carve("work", TT * AW).rearrange("p (t c) -> p t c", t=TT)
        og = carve("work", TT * REC).rearrange("p (t c) -> p t c", t=TT)
        s_b, p_b, pt_b = carve("work", 4 * 256), carve("work", 4 * 256), carve("work", 2 * 512)
        ysq = [carve("work", 512) for _ in range(2)]
        rt = carve("work", 512)
        asq, aacc = [s_b[:, 0:512], s_b[:, 512:1024]], p_b[:, 0:512]
        rec = [y.rearrange("p (t c) -> p t c", t=TT) for y in (y_k, y_q)]
        omix = ysq
        stage = carve("work", 3 * S, 4 * S).rearrange("p (n s) -> p n s", n=3)
        pre = carve("work", 3 + S)
        nat = carve("work", 2 * S)
        K_T, Q_T, K_n, V_n, Y_T, ATT, z_s = ([carve("work", S) for _ in range(2)] for _ in range(7))
        zraw, DS, gB, DD, o_t = (carve("work", S) for _ in range(5))
        XBT = carve("work", 2 * S)
        X, BT, nsq = XBT[:, 0:S], XBT[:, S:2 * S], XBT
        XT = nat[:, 0:S]
        U = carve("work", 256)
        state, nR, qsS, vnew, vdec = (carve("work", P) for _ in range(5))
        osq, oT, DI = sq[0], sq[1], acc

        rcol, rc_x, rc_t = carve("small", 16), carve("small", 16), carve("small", 16)
        ss, rs_, rs_t, mx = carve("small", 32), carve("small", 32), carve("small", 32), carve("small", 4)
        ang, kf, nang = carve("small", 8 * HR), carve("small", 8 * HR), carve("small", 8 * HR)
        C16 = carve("small", 8 * RD).rearrange("p (t e) -> p t e", t=8)
        S8 = carve("small", 8 * HR).rearrange("p (t e) -> p t e", t=8)
        N8 = carve("small", 8 * HR).rearrange("p (t e) -> p t e", t=8)
        mg, mge = carve("small", 24), carve("small", 24)
        mgn, mgd = carve("small", 8), carve("small", 8)
        absb = carve("small", 64, 16 * 3)
        dcol = carve("small", 6 * 32)
        g_c, t32a, t32b, t32c, u32, eb = (carve("small", 32) for _ in range(6))
        mx8 = carve("small", 8)
        hcol = [carve("small", 6 * TT) for _ in range(2)]
        cw = carve("small", 12)
        dss, drs, drt = carve("small", 8), carve("small", 8), carve("small", 8)
        oss, ors, ort = carve("small", 4), carve("small", 4), carve("small", 4)
        GC, NBETA, BETA, EGC, NBKD, CDEC = range(6)

        x_loaded, c_loaded, pos_loaded, ab_loaded = sem("x_loaded"), sem("c_loaded"), sem("pos_loaded"), sem("ab_loaded")
        p_loaded, out_stored = sem("p_loaded"), sem("out_stored")
        raw_loaded = [sem("raw_loaded0"), sem("raw_loaded1")]
        chunk_hi, chunk_lo = sem("chunk_hi"), sem("chunk_lo")
        tile_done, act_read, dve_read = sem("tile_done"), sem("act_read"), sem("dve_read")
        x_ready, h_hi, h_lo, sq_ready, acc_ready = sem("x_ready"), sem("h_hi"), sem("h_lo"), sem("sq_ready"), sem("acc_ready")
        ssq_full, sd_ready, rstd_ready = sem("ssq_full"), sem("sd_ready"), sem("rstd_ready")
        rcol_full, rcol_ready = sem("rcol_full"), sem("rcol_ready")
        relu_ready, hid_hi, relu2_ready, hid_lo = sem("relu_ready"), sem("hid_hi"), sem("relu2_ready"), sem("hid_lo")
        gate_sig, gate_mul = sem("gate_sig"), sem("gate_mul")
        p_hi, p_lo = sem("p_hi"), sem("p_lo")
        dve_step = sem("dve_step")
        trig_arg, trig_done = sem("trig_arg"), sem("trig_done")
        y_raw, ysq_read, y_gained, y_done = sem("y_raw"), sem("ysq_read"), sem("y_gained"), sem("y_done")
        qk_full, qk_placed = sem("qk_full"), sem("qk_placed")
        sc_full, sc_read, max_ready, p_ready = sem("sc_full"), sem("sc_read"), sem("max_ready"), sem("p_ready")
        pt_full, pt_placed, o_full, o_placed = sem("pt_full"), sem("pt_placed"), sem("o_full"), sem("o_placed")
        rec_stored = [sem("rec_stored0"), sem("rec_stored1")]
        rec_loaded = [sem("rec_loaded0"), sem("rec_loaded1")]
        mg_arg, mg_exp, mg_coef = sem("mg_arg"), sem("mg_exp"), sem("mg_coef")
        mg_others, omix_ready, pool_step = sem("mg_others"), sem("omix_ready"), sem("pool_step")
        mt_full, mt_hi, mt_lo = sem("mt_full"), sem("mt_hi"), sem("mt_lo")

        block = ctx.enter_context(nc.Block())

        def used_up(c):
            if c < C_AO:
                return 4 * (c + 1)
            if c < C_MLP[0]:
                return T_AO + 4 * (c - C_AO + 1)
            for layer in range(2):
                k = c - C_MLP[layer]
                if 0 <= k < 33:
                    return T_MLP[layer] + (2 * (k + 1) if k < 31 else 70 if k == 31 else 72)
                if 0 <= c - C_GATE[layer] < 4:
                    return T_GATE[layer] + 2 * (c - C_GATE[layer] + 1)
            return T_DO + 2 * (c - C_DO + 1)

        def split_hi(act, loads, slot, done=None, count=None):
            act.wait_ge(raw_loaded[slot], 16 * loads)
            if done is not None:
                act.wait_ge(done, count)
            nc.scalar.activation(w_hi[:, slot, :], raw[:, slot, :], ACT.Copy).then_inc(chunk_hi, 1)

        def split_lo(pool, c, slot):
            pool.wait_ge(chunk_hi, c + 1)
            nc.gpsimd.tensor_tensor(w_lo[:, slot, :], raw[:, slot, :], w_hi[:, slot, :].bitcast(F32),
                                    ALU.subtract).then_inc(chunk_lo, 1)

        def split_next(act, c):
            if c + 1 < N_CHUNKS:
                if c == 0:
                    split_hi(act, 1, 1)
                elif c == C_DO:
                    split_hi(act, (c + 1) // 2 + 1, (c + 1) % 2, dn_full, 4 * NH)
                else:
                    split_hi(act, (c + 1) // 2 + 1, (c + 1) % 2, tile_done, used_up(c - 1))

        def products(out_ap, lh, ll, rh, rl, start, stop):
            nc.tensor.matmul(out_ap, lh, rh, start=start, stop=False)
            nc.tensor.matmul(out_ap, lh, rl, start=False, stop=False)
            return nc.tensor.matmul(out_ap, ll, rh, start=False, stop=stop)

        def gemm_tile(pe, slot, n, width, t, bank, ks, hi, lo, k_ready=None):
            if isinstance(t, int) and t < T_AO + NB:
                pe.wait_ge(act_read, 36 - NB + (t - T_AO) + 1)
            else:
                pe.wait_ge(dve_read, t - T_AO - NB + 1)
            for k in range(ks):
                if k_ready is not None:
                    k_ready(k)
                a = k * width + n * P
                mm = products(pg[bank][:, :], w_hi[:, slot, a:a + P], w_lo[:, slot, a:a + P],
                              hi[:, k, :], lo[:, k, :], k == 0, k == ks - 1)
            mm.then_inc(tile_done, 1)

        NORM_BUF = [(A_hi, A_lo), (A_hi, A_lo), (A_hi, A_lo), (B_hi, B_lo), (B_hi, B_lo), (B_hi, B_lo)]
        ROW = {1: 1, 2: 2, 3: 3, 4: 4, 5: 5}

        def norm_sq(n):
            return (asq, aacc) if n == 0 else (sq, acc)

        def norm_act(act, n, k):
            e = n * KT + k + 1
            if n == 0:
                act.wait_ge(x_loaded, 16)
            else:
                act.wait_ge(*x_count(n, k))
            nc.scalar.activation(NORM_BUF[n][0][:, k, :], x[:, k, :], ACT.Copy,
                                 scale=Pm("gain", n * KT + k, n * KT + k + 1)).then_inc(h_hi, 1)
            if e > 2:
                act.wait_ge(acc_ready, e - 2)
            nc.scalar.activation(norm_sq(n)[0][k % 2], x[:, k, :], ACT.Square).then_inc(sq_ready, 1)

        def norm_lo(dve, n, k):
            dve.wait_ge(h_hi, n * KT + k + 1)
            hi, lo = NORM_BUF[n]
            nc.vector.scalar_tensor_tensor(lo[:, k, :], x[:, k, :], Pm("gain", n * KT + k, n * KT + k + 1),
                                           hi[:, k, :].bitcast(F32), ALU.mult, ALU.subtract).then_inc(h_lo, 1)

        def norm_sum(pool, n, k):
            squares, total = norm_sq(n)
            pool.wait_ge(sq_ready, n * KT + k + 1)
            if k == 0:
                if n in ROW and n > 1:
                    pool.wait_ge(ssq_full, ROW[n] - 1)
                nc.gpsimd.tensor_copy(total, squares[0]).then_inc(acc_ready, 1)
            else:
                pool.wait_ge(acc_ready, n * KT + k)
                nc.gpsimd.tensor_tensor(total, total, squares[k % 2], ALU.add).then_inc(acc_ready, 1)

        def norm_row_pe(pe, n):
            pe.wait_ge(acc_ready, (n + 1) * KT)
            if n == 1:
                pe.wait_ge(mt_lo, TT)
            nc.tensor.matmul(pa[0][:, :], ones, acc, start=True, stop=True).then_inc(ssq_full, 1)

        def norm_row_act(act, n):
            act.wait_ge(ssq_full, ROW[n])
            nc.scalar.activation(sdev, pa[0][:, :], ACT.Sqrt, scale=1.0 / D, bias=C("eps")).then_inc(sd_ready, 1)

        def norm_row_dve(dve, n):
            dve.wait_ge(sd_ready, ROW[n])
            nc.vector.reciprocal(rstd, sdev).then_inc(rstd_ready, 1)
            dve.wait_ge(rstd_ready, ROW[n])

        def tokens(row, d, j):
            return row[:, j:S:d] if d > 1 else row[:, j * P:(j + 1) * P]

        def norm_cols_pe(pe, n, strides):
            pe.wait_ge(acc_ready, (n + 1) * KT)
            for o, d in enumerate(strides):
                for j in range(TT):
                    mm = nc.tensor.matmul(pa[1][:, o * TT + j:o * TT + j + 1], tokens(norm_sq(n)[1], d, j),
                                          ones[:, 0:1], start=True, stop=True)
            mm.then_inc(rcol_full, 1)

        def norm_cols_dve(dve, link, count, nth):
            dve.wait_ge(rcol_full, nth)
            link(nc.vector.tensor_scalar(rc_x[:, 0:count], pa[1][:, 0:count], 1.0 / D, EPS, ALU.mult, ALU.add))
            rsqrt(nc.vector, link, rc_x[:, 0:count], rcol[:, 0:count], rc_t[:, 0:count], rcol_ready)

        UNITS = 2 * TT

        def key_blocks(gi, u):
            return 2 if GROUPS[gi][1] == 1 and u >= 2 else 1

        PT_BEFORE = {}
        total_pt = 0
        for gi in range(3):
            for u in range(UNITS):
                PT_BEFORE[gi, u] = total_pt
                total_pt += key_blocks(gi, u)
            PT_BEFORE[gi, UNITS] = total_pt

        SLOTS = 72
        TAIL = 14

        def riders(s):
            gi, r = divmod(s, 24)
            todo = []
            if gi < 3 and 13 <= r < 17:
                todo.append(("turn", gi, r - 13))
            if gi < 3 and r >= 20:
                todo.append(("turn", gi, 4 + r - 20))
            if 1 <= gi:
                if 3 <= r < 11:
                    todo.append(("values", gi - 1, r - 3))
                if 2 <= r < 10:
                    todo.append(("probs", gi - 1, r - 2))
                if gi == 3 and r % 2 == 0 and 4 <= r < 12:
                    todo.append(("merge", 3, (r - 4) // 2))
                if gi == 3 and 5 <= r and r % 2 == 1 and r < 13:
                    todo.append(("mix", 3, (r - 5) // 2))
                if r < 8:
                    todo.append(("scores", gi - 1, r))
            return todo

        @block.sync
        def _(sp):
            sp.dma_start(par[:, :], params).then_inc(c_loaded, 16)
            sp.dma_start(cst[:, :], consts).then_inc(c_loaded, 16)
            sp.dma_start(x[:, :, :], xT).then_inc(x_loaded, 16)
            for c in range(2):
                sp.dma_start(raw[:, c, :], weights[c, :, :]).then_inc(raw_loaded[c], 16)
            with sp.Fori(1, N_CHUNKS // 2) as m:
                for slot in range(2):
                    sp.wait_ge(chunk_lo, 2 * m + slot - 1)
                    sp.dma_start(raw[:, slot, :], weights[2 * m + slot, :, :]).then_inc(raw_loaded[slot], 16)
            for k in range(KT):
                sp.wait_ge(x_ready, KT + k + 1)
                sp.dma_start(out[:, k, :], x[:, k, :]).then_inc(out_stored, 16)
            sp.wait_ge(out_stored, 16 * KT)

        def x_count(n, k):
            if n in (1, 4):
                return dve_read, (0 if n == 1 else T_DO - T_AO) + k + 1
            if n in (2, 5):
                t = T_MLP[n // 4] + (56 + k if k < 6 else 70 + k - 6)
                return dve_read, t - T_AO + 1
            return x_ready, k + 1

        def pe_quarter(pe, layer, q, first=False, last=False):
            n, c0, t0 = 3 * layer + 1, C_MLP[layer], T_MLP[layer]
            din, hid = ((A_hi, A_lo), (B_hi, B_lo)) if layer == 0 else ((B_hi, B_lo), (A_hi, A_lo))
            for ck in range(4):
                pe.wait_ge(chunk_lo, c0 + 8 * q + ck + 1)
                for j in range(2):
                    gemm_tile(pe, (c0 + ck) % 2, j, 2 * P, t0 + 16 * q + 2 * ck + j, (2 * ck + j) % NB, KT, *din,
                              lambda k: pe.wait_ge(h_lo, n * KT + k + 1) if first and ck == 0 and j == 0 else None)
                    if first and ck == 0 and j == 0:
                        norm_row_pe(pe, n)
            for ck in range(4):
                if last and ck == 3:
                    t = t0 + 62
                    pe.wait_ge(chunk_lo, c0 + 31 + 1)
                    pe.wait_ge(p_lo, layer + 1)
                    for j in range(KT):
                        gemm_tile(pe, (c0 + 31) % 2, j, KT * P, t + j, (t + j) % NB, 2, din[0][:, 6:8, :], din[1][:, 6:8, :])
                c, t = c0 + 4 + ck, t0 + 16 * q + 8 + 2 * ck
                if last and ck == 3:
                    c, t = c0 + 32 - 8 * q, t0 + 70
                pe.wait_ge(chunk_lo, c + 8 * q + 1)
                for j in range(2):
                    gemm_tile(pe, c % 2, j, 2 * P, t + j, ((2 * ck if not (last and ck == 3) else 70) + j) % NB, KT, *hid,
                              lambda k: pe.wait_ge(hid_lo, 32 * layer + 8 * q + k + 1) if ck == 0 and j == 0 else None)

        def pe_tail(pe, layer):
            pe_quarter(pe, layer, 0, first=True)
            with pe.Fori(1, 3) as q:
                pe_quarter(pe, layer, q)
            pe_quarter(pe, layer, 3, last=True)
            n, din = 3 * layer + 2, NORM_BUF[3 * layer + 2]
            for ck in range(4):
                c, t = C_GATE[layer] + ck, T_GATE[layer] + 2 * ck
                pe.wait_ge(chunk_lo, c + 1)
                for j in range(2):
                    gemm_tile(pe, c % 2, j, 2 * P, t + j, (t + j) % NB, KT, *din,
                              lambda k: pe.wait_ge(h_lo, n * KT + k + 1) if ck == 0 and j == 0 else None)
                    if ck == 0 and j == 0:
                        norm_row_pe(pe, n)

        def turn(bank, src):
            for a in range(4):
                mm = nc.tensor.transpose(bank[:, a * P:(a + 1) * P], src[:, a * P:(a + 1) * P], ident)
            return mm

        def pe_attention(pe, kind, gi, u):
            j, half, n = u // 2, u % 2, gi * UNITS + u
            if kind == "turn":
                m = gi * 8 + u
                pe.wait_ge(y_done, gi * 2 + u // 4 + 1)
                wait(pe, qk_placed, m)
                if gi and u == 0:
                    pe.wait_ge(pt_placed, PT_BEFORE[gi - 1, UNITS])
                turn(pa[2], (y_k, y_q)[u // 4][:, (u % 4) * AW:(u % 4 + 1) * AW]).then_inc(qk_full, 1)
            elif kind == "scores":
                if u == 0:
                    pe.wait_ge(qk_placed, (gi + 1) * 8)
                wait(pe, sc_read, 2 * n)
                wide = key_blocks(gi, u) == 2
                k0, kw = ((j - 1) * P, 2 * P) if wide else (j * P, P)
                for b in range(2):
                    for a in range(2):
                        rows = slice(b * HD, (b + 1) * HD)
                        mm = nc.tensor.matmul(pa[b][:, a * 256:a * 256 + kw], qT[rows, 2 * half + a, j * P:(j + 1) * P],
                                              kT[rows, 2 * half + a, k0:k0 + kw], start=True, stop=True)
                mm.then_inc(sc_full, 1)
            elif kind == "probs":
                pe.wait_ge(p_ready, 4 * (n + 1))
                for b in range(key_blocks(gi, u)):
                    wait(pe, pt_placed, PT_BEFORE[gi, u] + b)
                    for h in range(4):
                        mm = nc.tensor.transpose(pa[2][:, h * P:(h + 1) * P],
                                                 p_b[:, h * 256 + b * P:h * 256 + (b + 1) * P], ident)
                    mm.then_inc(pt_full, 1)
            elif kind == "values":
                blocks = key_blocks(gi, u)
                pe.wait_ge(pt_placed, PT_BEFORE[gi, u] + blocks)
                pe.wait_ge(act_read, (gi + 1) * 3 * TT)
                if half == 0:
                    wait(pe, o_placed, gi * TT + j)
                for h in range(4):
                    hh = 4 * half + h
                    for b in range(blocks):
                        mm = nc.tensor.matmul(pa[3][:, hh * HD:(hh + 1) * HD],
                                              pt_b[:, b * 512 + h * P:b * 512 + (h + 1) * P],
                                              V[:, j - blocks + 1 + b, hh * HD:(hh + 1) * HD],
                                              start=(b == 0), stop=(b == blocks - 1))
                mm.then_inc(o_full, 1)
            elif kind == "mix":
                pe.wait_ge(omix_ready, u + 1)
                turn(pg[u], omix[u % 2]).then_inc(mt_full, 1)

        def pe_head(pe, i, par_, g, inv, scan):
            h, hi_, hs = i, i - 1, i - 2
            PA, PB, pI = pg[2], pg[3], pa[0]
            pv = 1 - par_
            for s in range(32):
                if g:
                    n, k = divmod(s, KT)
                    if k == 0:
                        if n % 2 == 0:
                            pe.wait_ge(chunk_lo, C_DN + 2 * h + n // 2 + 1)
                        wait(pe, dn_read, 4 * h + n - 1)
                    a = k * 2 * P + (n % 2) * P
                    sl = (C_DN + n // 2) % 2
                    mm = products(pg[n % 2][:, :], w_hi[:, sl, a:a + P], w_lo[:, sl, a:a + P], B_hi[:, k, :], B_lo[:, k, :],
                                  k == 0, k == KT - 1)
                    if k == KT - 1:
                        mm.then_inc(dn_full, 1)
                if inv:
                    if s == 0:
                        pe.wait_ge(dn_silu, 4 * hi_ + 2)
                        wait(pe, XT_placed, LEVELS * hi_)
                        wait(pe, att_done, hi_)
                        turn(PA, stage[:, 0, :]).then_inc(tq_full, 1)
                        turn(PB, stage[:, 1, :]).then_inc(tk_full, 1)
                    if s == 3:
                        pe.wait_ge(dn_silu, 4 * hi_ + 3)
                        pe.wait_ge(nq_placed, hi_ + 1)
                        turn(PA, stage[:, 2, :]).then_inc(tv_full, 1)
                        pe.wait_ge(nk_placed, hi_ + 1)
                        pe.wait_ge(gB_ready, hi_ + 1)
                        for t in range(TT):
                            mm = nc.tensor.matmul(PB[:, t * P:(t + 1) * P], gB[:, t * P:(t + 1) * P], C("incl"), start=True, stop=True)
                        mm.then_inc(gcb_full, 1)
                    if s == 9:
                        pe.wait_ge(v_placed, hi_ + 1)
                        pe.wait_ge(kn_ready, hi_ + 1)
                        turn(PA, K_n[pv]).then_inc(tkn_full, 1)
                        pe.wait_ge(dd_ready, hi_ + 1)
                        pe.wait_ge(qn_ready, hi_ + 1)
                        turn(PB, nat[:, 0:S]).then_inc(tqn_full, 1)
                    if s == 11:
                        pe.wait_ge(KT_placed, hi_ + 1)
                        for t in range(TT):
                            b = slice(t * P, (t + 1) * P)
                            mm = nc.tensor.matmul(PA[:, b], K_T[pv][:, b], K_T[pv][:, b], start=True, stop=True)
                        mm.then_inc(G_full, 1)
                        pe.wait_ge(QT_placed, hi_ + 1)
                        for t in range(TT):
                            b = slice(t * P, (t + 1) * P)
                            mm = nc.tensor.matmul(PB[:, b], K_T[pv][:, b], Q_T[pv][:, b], start=True, stop=True)
                        mm.then_inc(QK_full, 1)
                    for what, l in inverse_steps(s):
                        bs = 1 << l
                        if what == "U":
                            if l == 0:
                                pe.wait_ge(BT_ready, hi_ + 1)
                            wait(pe, X_done, LEVELS * hi_ + l)
                            for t in range(TT):
                                src = ident if l == 0 else X[:, t * P:(t + 1) * P]
                                mm = nc.tensor.matmul(pI[:, t * 64:(t + 1) * 64], BT[:, t * P:(t + 1) * P], even(src, bs),
                                                      start=True, stop=True)
                            mm.then_inc(U_full, 1)
                        elif what == "XU":
                            pe.wait_ge(U_placed, LEVELS * hi_ + l + 1)
                            pe.wait_ge(XT_placed, LEVELS * hi_ + l)
                            for t in range(TT):
                                mm = nc.tensor.matmul(pI[:, 256 + t * 64:256 + (t + 1) * 64], XT[:, t * P:(t + 1) * P],
                                                      U[:, t * 64:(t + 1) * 64], start=True, stop=True)
                            mm.then_inc(XU_full, 1)
                        else:
                            pe.wait_ge(X_done, LEVELS * hi_ + l + 1)
                            wait(pe, XT_placed, LEVELS * hi_ + l)
                            turn(PA, X).then_inc(XT_full, 1)
                if scan:
                    tt, st = divmod(s - 1, 7)
                    b = slice(tt * P, (tt + 1) * P)
                    if s >= 1 and tt < TT and st == 0:
                        if tt == 0:
                            pe.wait_ge(XT_placed, LEVELS * (hs + 1))
                        pe.wait_ge(state_ready, 4 * hs + tt + 1)
                        nc.tensor.matmul(pa[1][:, 0:P], K_T[par_][:, b], state, start=True, stop=True).then_inc(KS_full, 1)
                        wait(pe, qs_ready, 4 * hs + tt)
                        if tt == 0:
                            wait(pe, oT_ready, hs)
                        nc.tensor.matmul(pa[3][:, 0:P], Q_T[par_][:, b], state, start=True, stop=True).then_inc(QS_full, 1)
                    if s >= 1 and tt < TT and st == 2:
                        pe.wait_ge(nR_ready, 4 * hs + tt + 1)
                        wait(pe, o_done, 4 * hs + tt)
                        nc.tensor.matmul(pa[2][:, 0:P], Y_T[par_][:, b], nR, start=True, stop=True).then_inc(YR_full, 1)
                    if s >= 1 and tt < TT and st == 4:
                        pe.wait_ge(vn_ready, 4 * hs + tt + 1)
                        nc.tensor.matmul(pa[2][:, P:2 * P], ATT[par_][:, b], vnew, start=True, stop=True).then_inc(O_full, 1)
                        if tt < TT - 1:
                            pe.wait_ge(vd_ready, 3 * hs + tt + 1)
                            nc.tensor.matmul(pa[1][:, P:2 * P], K_n[par_][:, b], vdec, start=True, stop=True).then_inc(SN_full, 1)
                    if s == 30:
                        pe.wait_ge(on_ready, hs + 1)
                        pe.wait_ge(qs_ready, 4 * hs + 4)
                        turn(pa[3], o_t).then_inc(oT_full, 1)

        (dn_full, dn_read, dn_silu, dn_tap, dn_conv, tq_full, tk_full, tv_full, gcb_full, tkn_full, tqn_full,
         G_full, QK_full, nq_placed, nk_placed, v_placed, KT_placed, QT_placed, gB_ready, dd_ready, D_ready, DS_ready,
         DI_ready, nsq_ready, nsq_read, kn_ready, qn_ready, BT_ready, att_done, X_init, X_done, U_full, U_placed,
         XU_full, XT_full, XT_placed, KS_full, QS_full, YR_full, O_full, SN_full, nR_ready, qs_ready, vn_ready,
         vd_ready, o_done, state_ready, osq_ready, on_ready, oT_full, oT_ready, oT_hi, oT_lo) = (
            sem(n) for n in """dn_full dn_read dn_silu dn_tap dn_conv tq_full tk_full tv_full gcb_full
            tkn_full tqn_full G_full QK_full nq_placed nk_placed v_placed KT_placed QT_placed gB_ready dd_ready D_ready
            DS_ready DI_ready nsq_ready nsq_read kn_ready qn_ready BT_ready att_done X_init X_done U_full U_placed
            XU_full XT_full XT_placed KS_full QS_full YR_full O_full SN_full nR_ready qs_ready vn_ready vd_ready o_done
            state_ready osq_ready on_ready oT_full oT_ready oT_hi oT_lo""".split())
        ab_split, ab_full, g_arg, g_exp, g_ready, gc_full, gc_ready, g_cols = (
            sem(n) for n in "ab_split ab_full g_arg g_exp g_ready gc_full gc_ready g_cols".split())
        gemm_link, inv_link, scan_link = sem("gemm_link"), sem("inv_link"), sem("scan_link")
        GEMM_LINKS, INV_LINKS, SCAN_LINKS = 7, 14, 13

        def even(m, b):
            return m.rearrange("p (a two b) -> p a two b", two=2, b=b)[:, :, 0, :]

        def even4(m, b):
            return m.rearrange("p (a two b) -> p a two b", two=2, b=b)[:, :, 0, :]

        INV = [[("U", 0)], [("T", 0), ("U", 1)]]
        for _l in range(1, LEVELS):
            INV.append([("XU", _l)])
            INV.append([("T", _l)] + ([("U", _l + 1)] if _l + 1 < LEVELS else []))
        INV_SLOT = [13 + (j * 18) // (len(INV) - 1) for j in range(len(INV))]

        def inverse_steps(s):
            return [x_ for j, st in enumerate(INV) if INV_SLOT[j] == s for x_ in st]

        @block.tensor
        def _(pe):
            pe.wait_ge(c_loaded, 32)
            norm_cols_pe(pe, 0, (4, 1))
            pe.wait_ge(h_lo, KT)
            for s in range(SLOTS + TAIL):
                if s < SLOTS:
                    sec, half, tt = s // 8, (s // 4) % 2, s % 4
                    c, d = 2 * sec + half, GROUPS[sec // 3][1]
                    if tt == 0:
                        pe.wait_ge(chunk_lo, c + 1)
                    if half == 0:
                        wait(pe, act_read, (sec - 1) * TT + tt + 1)
                    for kk in range(4):
                        k = half * 4 + kk
                        mm = products(pg[tt][:, :], tokens(A_hi[:, k, :], d, tt), tokens(A_lo[:, k, :], d, tt),
                                      w_hi[:, c % 2, kk * 512:(kk + 1) * 512], w_lo[:, c % 2, kk * 512:(kk + 1) * 512],
                                      k == 0, k == KT - 1)
                    mm.then_inc(tile_done, 1)
                for kind, gi, u in riders(s):
                    pe_attention(pe, kind, gi, u)
            for ck in range(2):
                pe.wait_ge(chunk_lo, C_AO + ck + 1)
                if ck == 0:
                    pe.wait_ge(mt_lo, TT)
                for j in range(4):
                    t = T_AO + 4 * ck + j
                    gemm_tile(pe, ck, j, 4 * P, t, t % NB, 4, B_hi, B_lo)
            pe_tail(pe, 0)
            norm_cols_pe(pe, 3, (1,))
            pe.wait_ge(h_lo, 4 * KT)
            pe.wait_ge(ab_split, 2)
            for tt in range(TT):
                for k in range(KT):
                    b = slice(tt * P, (tt + 1) * P)
                    mm = products(pa[2][:, tt * 16:(tt + 1) * 16], B_hi[:, k, b], B_lo[:, k, b], ab_hi[:, k, :], ab_lo[:, k, :],
                                  k == 0, k == KT - 1)
            mm.then_inc(ab_full, 1)
            norm_row_pe(pe, 3)
            pe.wait_ge(dve_read, T_DO - T_AO)
            pe_head(pe, 0, 0, True, False, False)
            pe.wait_ge(g_ready, 1)
            nc.tensor.matmul(pa[2][:, 64:96], C("incl"), g_c, start=True, stop=True)
            nc.tensor.matmul(pa[2][:, 96:128], ones, g_c, start=True, stop=True).then_inc(gc_full, 1)
            pe_head(pe, 1, 1, True, True, False)
            with pe.Fori(1, NH // 2) as m:
                pe_head(pe, 2 * m, 0, True, True, True)
                pe_head(pe, 2 * m + 1, 1, True, True, True)
            pe_head(pe, NH, 0, False, True, True)
            pe_head(pe, NH + 1, 1, False, False, True)
            pe.wait_ge(oT_lo, NH)
            for ck in range(4):
                c, t = C_DO + ck, T_DO + 2 * ck
                pe.wait_ge(chunk_lo, c + 1)
                for j in range(2):
                    gemm_tile(pe, c % 2, j, 2 * P, t + j, (t + j) % NB, KT, A_hi, A_lo)
            pe_tail(pe, 1)

        def act_quarter(act, layer, q, last=False):
            n, c0, t0 = 3 * layer + 1, C_MLP[layer], T_MLP[layer]
            din, hid = (A_hi, B_hi) if layer == 0 else (B_hi, A_hi)
            for ck in range(4):
                k = 8 * q + ck
                split_hi(act, (c0 + ck + 1) // 2 + 1 + 4 * q, (c0 + ck + 1) % 2, tile_done, t0 + 2 * k)
                for j in range(2):
                    act.wait_ge(dve_read, t0 + 16 * q + 2 * ck + j - T_AO + 1)
                    nc.scalar.activation(hid[:, 2 * ck + j, :], relu[j], ACT.Square).then_inc(hid_hi, 1)
            if last:
                act.wait_ge(p_loaded, 16 * (layer + 1))
                act.wait_ge(tile_done, t0 + 56)
                nc.scalar.activation(din[:, 6:8, :], p_raw, ACT.Copy).then_inc(p_hi, 1)
            for ck in range(4):
                if last:
                    for cc in ([c0 + 28 + ck] if ck < 3 else [c0 + 31, c0 + 32]):
                        split_next(act, cc)
                    for j in range(2):
                        norm_act(act, n + 1, 2 * ck + j)
                else:
                    k = 8 * q + 4 + ck
                    split_hi(act, (c0 + 4 + ck + 1) // 2 + 1 + 4 * q, (c0 + ck + 1) % 2, tile_done, t0 + 2 * k)

        def act_tail(act, layer):
            n = 3 * layer + 1
            act.wait_ge(dve_read, (0, T_DO - T_AO)[layer] + KT)
            act.dma_start(p_raw, pT[:, layer * 1024:(layer + 1) * 1024]).then_inc(p_loaded, 16)
            norm_row_act(act, n)
            act_quarter(act, layer, 0)
            with act.Fori(1, 3) as q:
                act_quarter(act, layer, q)
            act_quarter(act, layer, 3, last=True)
            norm_row_act(act, n + 1)
            for ck in range(4):
                split_next(act, C_GATE[layer] + ck)
                for j in range(2):
                    k = 2 * ck + j
                    act.wait_ge(dve_read, T_GATE[layer] - T_AO + k + 1)
                    wait(act, x_ready, 8 * layer + k - 1)
                    nc.scalar.activation(act2[j], relu[j], ACT.Sigmoid).then_inc(gate_sig, 1)
                    if layer == 0 and k:
                        norm_act(act, 3, k - 1)
            if layer == 0:
                norm_act(act, 3, KT - 1)

        def act_attention(act, kind, gi, u):
            j, half, n = u // 2, u % 2, gi * UNITS + u
            if kind == "scores":
                kw = key_blocks(gi, u) * P
                act.wait_ge(max_ready, n + 1)
                wait(act, pt_full, PT_BEFORE[gi, u])
                for h in range(4):
                    hh = 4 * half + h
                    nc.scalar.activation(p_b[:, h * 256:h * 256 + kw], s_b[:, h * 256:h * 256 + kw], ACT.Exp,
                                         bias=og[:, j, AW + hh:AW + hh + 1], scale=ASCALE,
                                         accum_out=og[:, j, AW + AH + hh:AW + AH + hh + 1]).then_inc(p_ready, 1)
            elif kind == "values" and half == 1:
                act.wait_ge(o_full, n + 1)
                nc.scalar.activation(og[:, j, 0:AW], pa[3][:, :], ACT.Copy).then_inc(o_placed, 1)
                if gi < 2 and u == UNITS - 1:
                    act.wait_ge(o_placed, (gi + 1) * TT)
                    act.wait_ge(p_ready, 4 * (gi + 1) * UNITS)
                    for b in range(TT):
                        act.dma_start(scratch[gi].rearrange("(l r) c -> r l c", r=4)[b], og[:, b, :]).then_inc(rec_stored[gi], 16)
            elif kind == "merge":
                act.wait_ge(mg_arg, u + 1)
                nc.scalar.activation(mge, mg, ACT.Exp).then_inc(mg_exp, 1)
            elif kind == "mix":
                act.wait_ge(mt_full, u + 1)
                nc.scalar.activation(B_hi[:, 0:4, u * P:(u + 1) * P], pg[u][:, :].rearrange("p (a t) -> p a t", a=4),
                                     ACT.Copy).then_inc(mt_hi, 1)

        def act_head(act, i, par_, g, inv, scan):
            h, hi_, hs = i, i - 1, i - 2
            PA, PB = pg[2], pg[3]
            pv = 1 - par_
            for s in range(32):
                if g and s == 0:
                    if isinstance(h, int) and h == 0:
                        split_hi(act, 30, 0, tile_done, T_DO)
                    else:
                        split_hi(act, 30 + h, 0, dn_full, 4 * h)
                if g and s == 16:
                    split_hi(act, 30 + h, 1, dn_full, 4 * h + 2)
                if inv:
                    if s == 0:
                        act.wait_ge(tq_full, hi_ + 1)
                        nc.scalar.activation(nat[:, 0:S], PA[:, :], ACT.Copy).then_inc(nq_placed, 1)
                        act.wait_ge(tk_full, hi_ + 1)
                        nc.scalar.activation(nat[:, S:2 * S], PB[:, :], ACT.Copy).then_inc(nk_placed, 1)
                    if s == 3:
                        act.wait_ge(tv_full, hi_ + 1)
                        nc.scalar.activation(V_n[pv], PA[:, :], ACT.Copy).then_inc(v_placed, 1)
                    if s == 5:
                        act.wait_ge(dd_ready, hi_ + 1)
                        nc.scalar.activation(DD, DD, ACT.Exp).then_inc(D_ready, 1)
                    if s == 9:
                        act.wait_ge(tkn_full, hi_ + 1)
                        nc.scalar.activation(K_T[pv], PA[:, :], ACT.Copy).then_inc(KT_placed, 1)
                        act.wait_ge(tqn_full, hi_ + 1)
                        nc.scalar.activation(Q_T[pv], PB[:, :], ACT.Copy).then_inc(QT_placed, 1)
                    for what, l in inverse_steps(s):
                        if what == "T":
                            act.wait_ge(XT_full, LEVELS * hi_ + l + 1)
                            nc.scalar.activation(Y_T[pv] if l == LEVELS - 1 else XT, PA[:, :], ACT.Copy).then_inc(XT_placed, 1)
                if scan:
                    tt, st = divmod(s - 1, 7)
                    if s >= 1 and tt < TT and st == 0:
                        act.wait_ge(QS_full, 4 * hs + tt + 1)
                        wait(act, o_done, 4 * hs + tt)
                        nc.scalar.activation(qsS, pa[3][:, 0:P], ACT.Copy,
                                             scale=hcol[par_][:, EGC * TT + tt:EGC * TT + tt + 1]).then_inc(qs_ready, 1)
                    if s == 31:
                        act.wait_ge(oT_ready, hs + 1)
                        nc.scalar.activation(A_hi[:, hs, :], oT, ACT.Copy).then_inc(oT_hi, 1)
                if g and s % KT == KT - 1 and s < 24:
                    n = s // KT
                    act.wait_ge(dn_read, 4 * h + n + 1)
                    if n == 0:
                        wait(act, tq_full, h)
                    elif n == 1:
                        wait(act, tk_full, h)
                    else:
                        wait(act, tv_full, h)
                    nc.scalar.activation(stage[:, n, :], pre[:, 3:3 + S], ACT.Copy,
                                         scale=cw[:, 4 * n + 3:4 * n + 4]).then_inc(dn_tap, 1)
                if g and s in (10, 18, 26):
                    n = (s - 10) // KT
                    act.wait_ge(dn_conv, 3 * h + n + 1)
                    nc.scalar.activation(stage[:, n, :], stage[:, n, :], ACT.Silu).then_inc(dn_silu, 1)
                if g and s == 31:
                    act.wait_ge(dn_read, 4 * h + 4)
                    nc.scalar.activation(z_s[par_], zraw, ACT.Silu).then_inc(dn_silu, 1)

        @block.scalar
        def _(act):
            act.dma_start(posi[:, :], pos).then_inc(pos_loaded, 16)
            act.dma_start(rt[:, 0:KT * 16], wab).then_inc(ab_loaded, 16)
            act.wait_ge(c_loaded, 32)
            for k in range(KT):
                norm_act(act, 0, k)
            split_hi(act, 1, 0)
            act.wait_ge(ab_loaded, 16)
            nc.scalar.activation(ab_hi[:, :, :], rt[:, 0:KT * 16].rearrange("p (k c) -> p k c", c=16), ACT.Copy).then_inc(ab_split, 1)
            act.wait_ge(trig_arg, 2)
            nc.scalar.activation(S8[:, :, :], ang.rearrange("p (t e) -> p t e", t=8), ACT.Sin).then_inc(trig_done, 1)
            nc.scalar.activation(C16[:, :, 0:HR], nang.rearrange("p (t e) -> p t e", t=8), ACT.Sin).then_inc(trig_done, 1)
            for s in range(SLOTS + TAIL):
                if s < SLOTS:
                    sec, half, tt = s // 8, (s // 4) % 2, s % 4
                    if tt == 0:
                        split_next(act, 2 * sec + half)
                    if half == 1:
                        gi, what = divmod(sec, 3)
                        r0 = rcol[:, (TT if GROUPS[gi][1] == 1 else 0) + tt:][:, 0:1]
                        act.wait_ge(tile_done, 4 * (2 * sec + 1) + tt + 1)
                        if s < 8:
                            act.wait_ge(rcol_ready, 1)
                        if what == 2:
                            if gi and tt == 0:
                                act.wait_ge(o_full, gi * UNITS)
                            nc.scalar.activation(V[:, tt, :], pg[tt][:, :], ACT.Copy, scale=r0).then_inc(act_read, 1)
                        else:
                            n = (gi * 2 + what) * TT + tt
                            if gi:
                                act.wait_ge(qk_full, (gi - 1) * 8 + 4 * (what + 1))
                            nc.scalar.activation((y_k, y_q)[what][:, tt * AW:(tt + 1) * AW], pg[tt][:, :], ACT.Copy,
                                                 scale=r0).then_inc(y_raw, 1)
                            wait(act, ysq_read, n - 1)
                            nc.scalar.activation(ysq[tt % 2], pg[tt][:, :], ACT.Square, scale=r0).then_inc(act_read, 1)
                for kind, gi, u in riders(s):
                    act_attention(act, kind, gi, u)
                if s == SLOTS:
                    for g_ in range(2):
                        act.wait_ge(rec_stored[g_], 16 * TT)
                        act.wait_ge(qk_full, 16 + 4 * (g_ + 1))
                        act.dma_start(rec[g_], scratch[g_].rearrange("(t p) c -> p t c", p=P)).then_inc(rec_loaded[g_], 16)
            for ck in range(2):
                split_next(act, C_AO + ck)
                for j in range(4):
                    norm_act(act, 1, 4 * ck + j)
            act_tail(act, 0)
            act.wait_ge(g_arg, 1)
            nc.scalar.activation(t32c, t32b, ACT.Exp).then_inc(g_exp, 1)
            nc.scalar.activation(mx8, Pm("alog"), ACT.Exp).then_inc(g_exp, 1)
            nc.scalar.activation(eb, t32a, ACT.Exp).then_inc(g_exp, 1)
            act.wait_ge(g_exp, 3)
            nc.scalar.activation(t32c, t32c, ACT.Ln, bias=1.0).then_inc(g_exp, 1)
            norm_row_act(act, 3)
            act_head(act, 0, 0, True, False, False)
            act.wait_ge(gc_ready, 1)
            nc.scalar.activation(dcol[:, EGC * 32:EGC * 32 + 32], dcol[:, GC * 32:GC * 32 + 32], ACT.Exp).then_inc(g_cols, 1)
            nc.scalar.activation(t32c, t32b, ACT.Exp).then_inc(g_cols, 1)
            nc.scalar.activation(dcol[:, CDEC * 32:CDEC * 32 + 32], t32a, ACT.Exp).then_inc(g_cols, 1)
            act_head(act, 1, 1, True, True, False)
            with act.Fori(1, NH // 2) as m:
                act_head(act, 2 * m, 0, True, True, True)
                act_head(act, 2 * m + 1, 1, True, True, True)
            act_head(act, NH, 0, False, True, True)
            act_head(act, NH + 1, 1, False, False, True)
            for ck in range(4):
                split_next(act, C_DO + ck)
                for j in range(2):
                    norm_act(act, 4, 2 * ck + j)
            act_tail(act, 1)

        def heads_view(t):
            return t.rearrange("p (h e) -> p h e", e=HD)

        def per_head(col, heads=AH):
            return col.unsqueeze(2).to_broadcast([P, heads, HD])

        def pool_quarter(pool, layer, q, last=False):
            c0, t0 = C_MLP[layer], T_MLP[layer]
            for ck in range(4):
                split_lo(pool, c0 + 8 * q + ck + 1, (c0 + ck + 1) % 2)
                for j in range(2):
                    e = 32 * layer + 8 * q + 2 * ck + j + 1
                    pool.wait_ge(dve_read, t0 + 16 * q + 2 * ck + j - T_AO + 1)
                    wait(pool, hid_lo, e - 2)
                    nc.gpsimd.tensor_tensor(act2[j], relu[j], relu[j], ALU.mult).then_inc(relu2_ready, 1)
            for ck in range(4):
                if last:
                    for cc in ([c0 + 28 + ck] if ck < 3 else [c0 + 31, c0 + 32]):
                        split_lo(pool, cc + 1, (cc + 1) % 2)
                    for j in range(2):
                        norm_sum(pool, 3 * layer + 2, 2 * ck + j)
                else:
                    split_lo(pool, c0 + 8 * q + 4 + ck + 1, (c0 + ck + 1) % 2)

        def pool_tail(pool, layer):
            pool_quarter(pool, layer, 0)
            with pool.Fori(1, 3) as q:
                pool_quarter(pool, layer, q)
            pool_quarter(pool, layer, 3, last=True)
            for ck in range(4):
                c = C_GATE[layer] + ck
                if c + 1 < N_CHUNKS:
                    split_lo(pool, c + 1, (c + 1) % 2)
                for j in range(2):
                    if layer == 0 and 2 * ck + j:
                        norm_sum(pool, 3, 2 * ck + j - 1)
            if layer == 0:
                norm_sum(pool, 3, KT - 1)

        def pool_head(pool, i, par_, g, inv, scan):
            h, hi_, hs = i, i - 1, i - 2
            for s in range(32):
                if g and s == 0:
                    split_lo(pool, C_DN + 2 * h + 1, 0)
                if g and s == 16:
                    split_lo(pool, C_DN + 2 * h + 2, 1)
                if inv:
                    if s == 2:
                        pool.wait_ge(nk_placed, hi_ + 1)
                        wait(pool, XT_placed, LEVELS * hi_)
                        nc.gpsimd.tensor_tensor(nsq, nat, nat, ALU.mult).then_inc(nsq_ready, 1)
                    if s == 6:
                        pool.wait_ge(D_ready, hi_ + 1)
                        wait(pool, att_done, hi_)
                        nc.gpsimd.tensor_tensor(bank4(DS), bank4(DD), four(C("strict")), ALU.mult).then_inc(DS_ready, 1)
                        nc.gpsimd.tensor_tensor(bank4(DI), bank4(DD), four(C("incl")), ALU.mult).then_inc(DI_ready, 1)
                    if s == 7:
                        pool.wait_ge(nsq_read, hi_ + 1)
                        nc.gpsimd.tensor_tensor(bank4(X), four(ident), four(ident), ALU.mult).then_inc(X_init, 1)
                if scan and s == 27:
                    pool.wait_ge(o_done, 4 * hs + 4)
                    nc.gpsimd.tensor_tensor(osq, o_t, o_t, ALU.mult).then_inc(osq_ready, 1)

        def bank4(t):
            return t.rearrange("p (t c) -> p t c", t=TT)

        def four(m, n=TT):
            return m.unsqueeze(1).to_broadcast([P, n, m.shape[1]])

        @block.gpsimd
        def _(pool):
            for k in range(KT):
                norm_sum(pool, 0, k)
            split_lo(pool, 0, 0)
            for s in range(SLOTS + TAIL):
                if s < SLOTS:
                    sec, half, tt = s // 8, (s // 4) % 2, s % 4
                    if tt == 0:
                        split_lo(pool, 2 * sec + half + 1, (half + 1) % 2)
                    gi, what = divmod(sec, 3)
                    if half == 1 and what < 2:
                        n = (gi * 2 + what) * TT + tt
                        pool.wait_ge(y_raw, n + 1)
                        y = heads_view((y_k, y_q)[what][:, tt * AW:(tt + 1) * AW])
                        gain = Pm("kg" if what == 0 else "qg", gi * HD, (gi + 1) * HD)
                        nc.gpsimd.tensor_tensor(y, y, four(gain, AH), ALU.mult).then_inc(y_gained, 1)
                for kind, _g, u in riders(s):
                    if kind == "merge":
                        pool.wait_ge(rec_loaded[0], 16)
                        pool.wait_ge(rec_loaded[1], 16)
                        pool.wait_ge(mg_coef, u + 1)
                        for g_ in range(2):
                            o_ = heads_view(rec[g_][:, u, 0:AW])
                            nc.gpsimd.tensor_tensor(o_, o_, per_head(mge[:, g_ * AH:(g_ + 1) * AH]), ALU.mult).then_inc(pool_step, 1)
                        pool.wait_ge(pool_step, 2 * u + 2)
                        nc.gpsimd.tensor_tensor(rec[0][:, u, 0:AW], rec[0][:, u, 0:AW], rec[1][:, u, 0:AW],
                                                ALU.add).then_inc(mg_others, 1)
            for ck in range(2):
                split_lo(pool, C_AO + ck + 1, (C_AO + ck + 1) % 2)
                for j in range(4):
                    norm_sum(pool, 1, 4 * ck + j)
            pool_tail(pool, 0)
            pool_head(pool, 0, 0, True, False, False)
            pool_head(pool, 1, 1, True, True, False)
            with pool.Fori(1, NH // 2) as m:
                pool_head(pool, 2 * m, 0, True, True, True)
                pool_head(pool, 2 * m + 1, 1, True, True, True)
            pool_head(pool, NH, 0, False, True, True)
            pool_head(pool, NH + 1, 1, False, False, True)
            for ck in range(4):
                split_lo(pool, C_DO + ck + 1, (C_DO + ck + 1) % 2)
                for j in range(2):
                    norm_sum(pool, 4, 2 * ck + j)
            pool_tail(pool, 1)

        def add_to_x(dve, t, bank, k):
            dve.wait_ge(tile_done, t + 1)
            nc.vector.tensor_tensor(x[:, k, :], x[:, k, :], pg[bank][:, :], ALU.add).then_inc(dve_read, 1)
            dve.wait_ge(dve_read, t - T_AO + 1)

        def dve_quarter(dve, layer, q, first=False, last=False):
            n, t0 = 3 * layer + 1, T_MLP[layer]
            hid = (B_hi, B_lo) if layer == 0 else (A_hi, A_lo)
            din = (A_hi, A_lo) if layer == 0 else (B_hi, B_lo)
            if first:
                norm_row_dve(dve, n)

            def low(k):
                e = 32 * layer + 8 * q + k + 1
                dve.wait_ge(hid_hi, e)
                dve.wait_ge(relu2_ready, e)
                nc.vector.tensor_tensor(hid[1][:, k, :], act2[k % 2], hid[0][:, k, :].bitcast(F32), ALU.subtract).then_inc(hid_lo, 1)

            for k in range(8):
                t = t0 + 16 * q + k
                e = 32 * layer + 8 * q + k + 1
                dve.wait_ge(tile_done, t + 1)
                wait(dve, hid_hi, e - 2)
                wait(dve, relu2_ready, e - 2)
                nc.vector.scalar_tensor_tensor(relu[k % 2], pg[k % NB][:, :], 0.0, rstd, ALU.max, ALU.mult).then_inc(dve_read, 1)
                if k:
                    low(k - 1)
            low(7)
            for k in range(8):
                t, bank = t0 + 16 * q + 8 + k, k % NB
                if last and k == 0:
                    dve.wait_ge(p_hi, layer + 1)
                    nc.vector.tensor_tensor(din[1][:, 6:8, :], p_raw, din[0][:, 6:8, :].bitcast(F32), ALU.subtract).then_inc(p_lo, 1)
                if last and k == 6:
                    for j in range(KT):
                        dve.wait_ge(tile_done, t0 + 62 + j + 1)
                        nc.vector.tensor_copy(ple[:, j, :], pg[(62 + j) % NB][:, :]).then_inc(dve_read, 1)
                if last and k >= 6:
                    t, bank = t0 + 70 + k - 6, (70 + k - 6) % NB
                add_to_x(dve, t, bank, k)
                if last and k:
                    norm_lo(dve, n + 1, k - 1)
            if last:
                norm_lo(dve, n + 1, 7)

        def dve_tail(dve, layer):
            dve_quarter(dve, layer, 0, first=True)
            with dve.Fori(1, 3) as q:
                dve_quarter(dve, layer, q)
            dve_quarter(dve, layer, 3, last=True)
            norm_row_dve(dve, 3 * layer + 2)

            def gated(k):
                dve.wait_ge(gate_sig, 8 * layer + k + 1)
                nc.vector.tensor_tensor(act2[k % 2], act2[k % 2], ple[:, k, :], ALU.mult).then_inc(gate_mul, 1)
                dve.wait_ge(gate_mul, 8 * layer + k + 1)
                nc.vector.tensor_tensor(x[:, k, :], x[:, k, :], act2[k % 2], ALU.add).then_inc(x_ready, 1)

            for k in range(KT):
                t = T_GATE[layer] + k
                dve.wait_ge(tile_done, t + 1)
                wait(dve, gate_sig, 8 * layer + k - 1)
                nc.vector.tensor_tensor(relu[k % 2], pg[k % NB][:, :], rstd, ALU.mult).then_inc(dve_read, 1)
                if k:
                    gated(k - 1)
                if layer == 0 and k > 1:
                    norm_lo(dve, 3, k - 2)
            gated(KT - 1)
            if layer == 0:
                norm_lo(dve, 3, KT - 2)
                norm_lo(dve, 3, KT - 1)

        def dve_attention(dve, link, kind, gi, u):
            j, half, n = u // 2, u % 2, gi * UNITS + u
            if kind == "turn":
                m = gi * 8 + u
                tt = u % 4
                dve.wait_ge(qk_full, m + 1)
                if gi and u % 4 == 0:
                    dve.wait_ge(sc_full, gi * UNITS)
                nc.vector.tensor_copy((kT, qT)[u // 4][:, :, tt * P:(tt + 1) * P],
                                      pa[2][:, :].rearrange("p (a t) -> p a t", a=4)).then_inc(qk_placed, 1)
            elif kind == "scores":
                wide = key_blocks(gi, u) == 2
                kw = 2 * P if wide else P
                mask = C("resid") if gi == 0 else C("band", 0 if wide else P)
                dve.wait_ge(sc_full, n + 1)
                wait(dve, p_ready, 4 * n)
                s4 = s_b.rearrange("p (a b c) -> p b a c", a=2, b=2)
                for b in range(2):
                    nc.vector.tensor_tensor(s4[:, b, :, 0:kw], pa[b][:, :].rearrange("p (a c) -> p a c", a=2)[:, :, 0:kw],
                                            four(mask, 2), ALU.add).then_inc(sc_read, 1)
                dve.wait_ge(sc_read, 2 * n + 2)
                link(nc.vector.tensor_reduce(mx, s_b.rearrange("p (h c) -> p h c", h=4)[:, :, 0:kw], AX, ALU.max))
                if n == gi * UNITS and gi:
                    dve.wait_ge(rec_stored[gi - 1], 16 * TT)
                nc.vector.tensor_scalar(og[:, j, AW + 4 * half:AW + 4 * half + 4], mx, -ASCALE, None, ALU.mult).then_inc(max_ready, 1)
            elif kind == "probs":
                for b in range(key_blocks(gi, u)):
                    m = PT_BEFORE[gi, u] + b
                    dve.wait_ge(pt_full, m + 1)
                    wait(dve, o_full, n)
                    nc.vector.tensor_copy(pt_b[:, b * 512:(b + 1) * 512], pa[2][:, :]).then_inc(pt_placed, 1)
            elif kind == "merge":
                if u == 0:
                    dve.wait_ge(rec_loaded[0], 16)
                    dve.wait_ge(rec_loaded[1], 16)
                dve.wait_ge(p_ready, 4 * (2 * UNITS + 2 * u + 2))
                recs = [rec[0][:, u, :], rec[1][:, u, :], og[:, u, :]]
                nm = [r[:, AW:AW + AH] for r in recs]
                den = [r[:, AW + AH:REC] for r in recs]
                wait(dve, mg_others, u)
                link(nc.vector.tensor_tensor(mgn, nm[0], nm[1], ALU.min))
                link(nc.vector.tensor_tensor(mgn, mgn, nm[2], ALU.min))
                for g_ in range(3):
                    ins = nc.vector.tensor_tensor(mg[:, g_ * AH:(g_ + 1) * AH], mgn, nm[g_], ALU.subtract)
                    link(ins) if g_ < 2 else ins.then_inc(mg_arg, 1)
                dve.wait_ge(mg_exp, u + 1)
                for g_ in range(3):
                    link(nc.vector.tensor_tensor(mg[:, g_ * AH:(g_ + 1) * AH], mge[:, g_ * AH:(g_ + 1) * AH], den[g_], ALU.mult))
                link(nc.vector.tensor_tensor(mgd, mg[:, 0:AH], mg[:, AH:2 * AH], ALU.add))
                link(nc.vector.tensor_tensor(mgd, mgd, mg[:, 2 * AH:3 * AH], ALU.add))
                link(nc.vector.reciprocal(mgd, mgd))
                nc.vector.tensor_tensor(mge.rearrange("p (g h) -> p g h", g=3), mge.rearrange("p (g h) -> p g h", g=3),
                                        mgd.unsqueeze(1).to_broadcast([P, 3, AH]), ALU.mult).then_inc(mg_coef, 1)
                dve.wait_ge(mg_coef, u + 1)
                dve.wait_ge(o_placed, 2 * TT + u + 1)
                wait(dve, mt_full, u - 1)
                link(nc.vector.tensor_tensor(heads_view(omix[u % 2]), heads_view(og[:, u, 0:AW]), per_head(mge[:, 2 * AH:3 * AH]), ALU.mult))
                dve.wait_ge(mg_others, u + 1)
                nc.vector.tensor_tensor(omix[u % 2], omix[u % 2], rec[0][:, u, 0:AW], ALU.add).then_inc(omix_ready, 1)
            elif kind == "mix":
                dve.wait_ge(mt_hi, u + 1)
                b = slice(u * P, (u + 1) * P)
                nc.vector.tensor_tensor(B_lo[:, 0:4, b], pg[u][:, :].rearrange("p (a t) -> p a t", a=4),
                                        B_hi[:, 0:4, b].bitcast(F32), ALU.subtract).then_inc(mt_lo, 1)

        def finish_y(dve, link, gi, what):
            n = gi * 2 + what
            y = (y_k, y_q)[what][:, 0:TT * AW]
            link(nc.vector.tensor_scalar(ss, ss, 1.0 / HD, EPS, ALU.mult, ALU.add))
            rsqrt(nc.vector, link, ss, rs_, rs_t)
            dve.wait_ge(y_gained, (n + 1) * TT)
            link(nc.vector.tensor_tensor(heads_view(y), heads_view(y), per_head(rs_, TT * AH), ALU.mult))
            y4 = y.rearrange("p (t h e) -> p t h e", t=TT, e=HD)
            r4 = rt.rearrange("p (t h e) -> p t h e", t=TT, e=RD)
            o = (TT if GROUPS[gi][1] == 1 else 0)

            def table(tab, w):
                return tab[:, o:o + TT, :].unsqueeze(2).to_broadcast([P, TT, AH, w])

            link(nc.vector.tensor_tensor(r4[:, :, :, 0:HR], y4[:, :, :, HR:RD], table(N8, HR), ALU.mult))
            link(nc.vector.tensor_tensor(r4[:, :, :, HR:RD], y4[:, :, :, 0:HR], table(S8, HR), ALU.mult))
            link(nc.vector.tensor_tensor(y4[:, :, :, 0:RD], y4[:, :, :, 0:RD], table(C16, RD), ALU.mult))
            nc.vector.tensor_tensor(y4[:, :, :, 0:RD], y4[:, :, :, 0:RD], r4, ALU.add).then_inc(y_done, 1)

        def rope_tables(dve, link):
            dve.wait_ge(pos_loaded, 16)
            link(nc.vector.tensor_copy(rc_t[:, 0:8], posi[:, :]))
            a3 = ang.rearrange("p (t e) -> p t e", t=8)
            link(nc.vector.tensor_tensor(a3, rc_t[:, 0:8].unsqueeze(2).to_broadcast([P, 8, HR]), four(C("freq"), 8), ALU.mult))
            link(nc.vector.tensor_scalar(kint[:, :], ang, 1.0 / (2 * np.pi), None, ALU.mult))
            link(nc.vector.tensor_copy(kf, kint[:, :]))
            c1 = 6.28125
            c2 = float(np.round((2 * np.pi - c1) * 2**20) / 2**20)
            c3 = float(np.float32(2 * np.pi - c1 - c2))
            for part in (c1, c2, c3):
                link(nc.vector.scalar_tensor_tensor(ang, kf, -part, ang, ALU.mult, ALU.add))
            lim = 3.1415925
            link(nc.vector.tensor_scalar(ang, ang, -lim, lim, ALU.max, ALU.min))
            nc.vector.tensor_scalar(kf, ang, -1.0, None, ALU.mult).then_inc(trig_arg, 1)
            dve.wait_ge(trig_arg, 1)
            link(nc.vector.tensor_tensor(kf, kf, ang, ALU.max))
            nc.vector.tensor_scalar(nang, kf, -1.0, float(np.pi / 2), ALU.mult, ALU.add).then_inc(trig_arg, 1)
            dve.wait_ge(trig_done, 2)
            link(nc.vector.tensor_scalar(N8[:, :, :], S8[:, :, :], -1.0, None, ALU.mult))
            link(nc.vector.tensor_copy(C16[:, :, HR:RD], C16[:, :, 0:HR]))

        def dve_head(dve, i, par_, g, inv, scan):
            h, hi_, hs = i, i - 1, i - 2
            pv = 1 - par_
            PA, PB, pI = pg[2], pg[3], pa[0]
            glink = Chain(dve, gemm_link, h * GEMM_LINKS)
            ilink = Chain(dve, inv_link, hi_ * INV_LINKS)
            slink = Chain(dve, scan_link, hs * SCAN_LINKS)

            def col(p_, q, t):
                return hcol[p_][:, q * TT + t:q * TT + t + 1]

            for s in range(32):
                if g and s == 0:
                    wait(dve, dn_conv, 3 * h)
                    glink(nc.vector.tensor_copy(cw, Pm("conv").rearrange("p (h c) -> p h c", c=12)[:, h, :]))
                if inv and s == 0:
                    wait(dve, o_done, 4 * hs)
                    wait(dve, state_ready, 4 * hs)
                    ilink(nc.vector.tensor_copy(hcol[pv], dcol.rearrange("p (q h) -> p q h", h=NH)[:, :, hi_]))
                    nc.vector.tensor_copy(bank4(gB), g_c.rearrange("p (t h) -> p t h", h=NH)[:, :, hi_].unsqueeze(2)
                                          .to_broadcast([P, TT, P])).then_inc(gB_ready, 1)
                if scan and s == 0:
                    nc.vector.memset(state, 0.0).then_inc(state_ready, 1)
                    dve.wait_ge(state_ready, 4 * hs + 1)
                if inv:
                    if s == 4:
                        dve.wait_ge(gcb_full, hi_ + 1)
                        wait(dve, DI_ready, hi_)
                        for t in range(TT):
                            b = slice(t * P, (t + 1) * P)
                            ins = nc.vector.tensor_scalar(DD[:, b], PB[:, b], col(pv, GC, t), 0.0, ALU.subtract, ALU.min)
                        ins.then_inc(dd_ready, 1)
                    if s == 5:
                        dve.wait_ge(nsq_ready, hi_ + 1)
                        nc.vector.tensor_reduce(dss, nsq.rearrange("p (n c) -> p n c", n=2 * TT), AX, ALU.add).then_inc(nsq_read, 1)
                        dve.wait_ge(nsq_read, hi_ + 1)
                        ilink(nc.vector.tensor_scalar(dss, dss, EPS, None, ALU.add))
                        rsqrt(nc.vector, ilink, dss, drs, drt)
                        ilink(nc.vector.tensor_scalar(drs[:, 0:TT], drs[:, 0:TT], QS, None, ALU.mult))
                        nc.vector.tensor_tensor(bank4(K_n[pv]), bank4(nat[:, S:2 * S]), drs[:, TT:2 * TT].unsqueeze(2)
                                                .to_broadcast([P, TT, P]), ALU.mult).then_inc(kn_ready, 1)
                        nc.vector.tensor_tensor(bank4(nat[:, 0:S]), bank4(nat[:, 0:S]), drs[:, 0:TT].unsqueeze(2)
                                                .to_broadcast([P, TT, P]), ALU.mult).then_inc(qn_ready, 1)
                    if s == 12:
                        dve.wait_ge(G_full, hi_ + 1)
                        dve.wait_ge(DS_ready, hi_ + 1)
                        for t in range(TT):
                            b = slice(t * P, (t + 1) * P)
                            ins = nc.vector.scalar_tensor_tensor(BT[:, b], PA[:, b], col(pv, BETA, t), DS[:, b], ALU.mult, ALU.mult)
                        ins.then_inc(BT_ready, 1)
                        dve.wait_ge(QK_full, hi_ + 1)
                        dve.wait_ge(DI_ready, hi_ + 1)
                        nc.vector.tensor_tensor(ATT[pv], PB[:, :], DI, ALU.mult).then_inc(att_done, 1)
                    for what, l in inverse_steps(s):
                        bs = 1 << l
                        if what == "U":
                            dve.wait_ge(U_full, LEVELS * hi_ + l + 1)
                            nc.vector.tensor_tensor(U.rearrange("p (t c) -> p t c", t=TT), pI[:, 0:256].rearrange("p (t c) -> p t c", t=TT),
                                                    four(C("lev", l * 64, (l + 1) * 64)), ALU.mult).then_inc(U_placed, 1)
                            dve.wait_ge(U_placed, LEVELS * hi_ + l + 1)
                        if (what, l) == ("U", 0):
                            dve.wait_ge(X_init, hi_ + 1)
                            ev = even(X, bs)
                            nc.vector.tensor_tensor(ev, ev, U.rearrange("p (a b) -> p a b", b=bs), ALU.subtract).then_inc(X_done, 1)
                            dve.wait_ge(X_done, LEVELS * hi_ + 1)
                        if what == "XU":
                            dve.wait_ge(XU_full, (LEVELS - 1) * hi_ + l)
                            ev = even(X, bs)
                            nc.vector.tensor_tensor(ev, ev, pI[:, 256:512].rearrange("p (a b) -> p a b", b=bs), ALU.subtract).then_inc(X_done, 1)
                            dve.wait_ge(X_done, LEVELS * hi_ + l + 1)
                if scan:
                    tt, st = divmod(s - 1, 7)
                    if s >= 1 and tt < TT:
                        b = slice(tt * P, (tt + 1) * P)
                        e = 4 * hs + tt + 1
                        if st == 0:
                            dve.wait_ge(KS_full, e)
                            nc.vector.scalar_tensor_tensor(nR, pa[1][:, 0:P], col(par_, EGC, tt), V_n[par_][:, b],
                                                           ALU.mult, ALU.subtract).then_inc(nR_ready, 1)
                        if st == 2:
                            dve.wait_ge(YR_full, e)
                            wait(dve, O_full, e - 1)
                            if tt < TT - 1:
                                nc.vector.tensor_scalar(vdec, pa[2][:, 0:P], col(par_, NBKD, tt), None, ALU.mult).then_inc(vd_ready, 1)
                            nc.vector.tensor_scalar(vnew, pa[2][:, 0:P], col(par_, NBETA, tt), None, ALU.mult).then_inc(vn_ready, 1)
                        if st == 4:
                            dve.wait_ge(O_full, e)
                            dve.wait_ge(qs_ready, e)
                            if tt == 0:
                                wait(dve, oT_full, hs)
                            nc.vector.tensor_tensor(o_t[:, b], pa[2][:, P:2 * P], qsS, ALU.add).then_inc(o_done, 1)
                            if tt < TT - 1:
                                dve.wait_ge(SN_full, 3 * hs + tt + 1)
                                nc.vector.scalar_tensor_tensor(state, state, col(par_, CDEC, tt), pa[1][:, P:2 * P],
                                                               ALU.mult, ALU.add).then_inc(state_ready, 1)
                                dve.wait_ge(state_ready, 4 * hs + tt + 2)
                    if s == 28:
                        dve.wait_ge(osq_ready, hs + 1)
                        slink(nc.vector.tensor_reduce(oss, bank4(osq), AX, ALU.add))
                        slink(nc.vector.tensor_scalar(oss, oss, 1.0 / P, EPS, ALU.mult, ALU.add))
                        rsqrt(nc.vector, slink, oss, ors, ort)
                        nc.vector.tensor_tensor(bank4(o_t), bank4(o_t), ors.unsqueeze(2).to_broadcast([P, TT, P]), ALU.mult).then_inc(on_ready, 1)
                    if s == 30:
                        dve.wait_ge(oT_full, hs + 1)
                        wait(dve, oT_hi, hs)
                        wait(dve, oT_lo, hs)
                        nc.vector.scalar_tensor_tensor(oT, pa[3][:, :], Pm("og"), z_s[par_], ALU.mult, ALU.mult).then_inc(oT_ready, 1)
                    if s == 31:
                        dve.wait_ge(oT_hi, hs + 1)
                        nc.vector.tensor_tensor(A_lo[:, hs, :], oT, A_hi[:, hs, :].bitcast(F32), ALU.subtract).then_inc(oT_lo, 1)
                if g and s % KT == KT - 1:
                    n = s // KT
                    dve.wait_ge(dn_full, 4 * h + n + 1)
                    if n < 3:
                        wait(dve, dn_tap, 3 * h + n)
                        wait(dve, dn_conv, 3 * h + n)
                        nc.vector.tensor_tensor(pre[:, 3:3 + S], pg[n % 2][:, :], rstd, ALU.mult).then_inc(dn_read, 1)
                        dve.wait_ge(dn_read, 4 * h + n + 1)
                        for tap in (2, 1, 0):
                            if tap == 2:
                                dve.wait_ge(dn_tap, 3 * h + n + 1)
                            ins = nc.vector.scalar_tensor_tensor(stage[:, n, :], pre[:, tap:tap + S], cw[:, 4 * n + tap:4 * n + tap + 1],
                                                                 stage[:, n, :], ALU.mult, ALU.add)
                            glink(ins) if tap else ins.then_inc(dn_conv, 1)
                    else:
                        wait(dve, dn_silu, 4 * h)
                        nc.vector.tensor_tensor(zraw, pg[n % 2][:, :], rstd, ALU.mult).then_inc(dn_read, 1)
            assert not g or glink.n == GEMM_LINKS, glink.n
            assert not inv or ilink.n == INV_LINKS, ilink.n
            assert not scan or slink.n == SCAN_LINKS, slink.n

        @block.vector
        def _(dve):
            link = Chain(dve, dve_step)
            dve.wait_ge(c_loaded, 32)
            for k in range(KT):
                norm_lo(dve, 0, k)
            norm_cols_dve(dve, link, 8, 1)
            dve.wait_ge(ab_split, 1)
            nc.vector.tensor_tensor(ab_lo[:, :, :], rt[:, 0:KT * 16].rearrange("p (k c) -> p k c", c=16), ab_hi[:, :, :].bitcast(F32),
                                    ALU.subtract).then_inc(ab_split, 1)
            dve.wait_ge(ab_split, 2)
            rope_tables(dve, link)
            for s in range(SLOTS + TAIL):
                if s < SLOTS:
                    sec, half, tt = s // 8, (s // 4) % 2, s % 4
                    gi, what = divmod(sec, 3)
                    if half == 1 and what < 2:
                        n = (gi * 2 + what) * TT + tt
                        dve.wait_ge(act_read, sec * TT + tt + 1)
                        nc.vector.tensor_reduce(ss[:, tt * AH:(tt + 1) * AH], heads_view(ysq[tt % 2]), AX, ALU.add).then_inc(ysq_read, 1)
                        dve.wait_ge(ysq_read, n + 1)
                    if s % 8 == 0 and 0 < what:
                        finish_y(dve, link, gi, what - 1)
                for kind, gi, u in riders(s):
                    dve_attention(dve, link, kind, gi, u)
            for k in range(KT):
                add_to_x(dve, T_AO + k, k % NB, k)
                if k:
                    norm_lo(dve, 1, k - 1)
            norm_lo(dve, 1, KT - 1)
            dve_tail(dve, 0)
            norm_cols_dve(dve, link, 4, 2)
            dve.wait_ge(rcol_ready, 2)
            dve.wait_ge(ab_full, 1)
            ab4 = absb.rearrange("p (t c) -> p t c", t=TT)
            link(nc.vector.tensor_tensor(ab4, pa[2][:, 0:64].rearrange("p (t c) -> p t c", t=TT),
                                         rcol[:, 0:TT].unsqueeze(2).to_broadcast([P, TT, 16]), ALU.mult))
            v4 = lambda t: t.rearrange("p (t h) -> p t h", t=TT)
            link(nc.vector.tensor_tensor(v4(u32), ab4[:, :, 0:NH], four(Pm("dt")), ALU.add))
            link(nc.vector.scalar_tensor_tensor(t32b, u32, -1.0, u32, ALU.mult, ALU.min))
            nc.vector.tensor_scalar(v4(t32a), ab4[:, :, NH:2 * NH], -87.0, -1.0, ALU.max, ALU.mult).then_inc(g_arg, 1)
            dve.wait_ge(g_exp, 4)
            link(nc.vector.scalar_tensor_tensor(u32, u32, 0.0, t32c, ALU.max, ALU.add))
            nc.vector.scalar_tensor_tensor(v4(g_c), v4(u32), -1.0, four(mx8), ALU.mult, ALU.mult).then_inc(g_ready, 1)
            link(nc.vector.tensor_scalar(eb, eb, 1.0, None, ALU.add))
            link(nc.vector.reciprocal(dcol[:, BETA * 32:BETA * 32 + 32], eb))
            link(nc.vector.tensor_scalar(dcol[:, NBETA * 32:NBETA * 32 + 32], dcol[:, BETA * 32:BETA * 32 + 32], -1.0, None, ALU.mult))
            norm_row_dve(dve, 3)
            link(nc.vector.memset(pre[:, 0:3], 0.0))
            dve_head(dve, 0, 0, True, False, False)
            dve.wait_ge(gc_full, 1)
            link(nc.vector.tensor_copy(dcol[:, GC * 32:GC * 32 + 32], pa[2][:, 64:96]))
            link(nc.vector.tensor_copy(t32a, pa[2][:, 96:128]))
            nc.vector.tensor_tensor(t32b, t32a, dcol[:, GC * 32:GC * 32 + 32], ALU.subtract).then_inc(gc_ready, 1)
            dve.wait_ge(g_cols, 3)
            link(nc.vector.tensor_tensor(dcol[:, NBKD * 32:NBKD * 32 + 32], dcol[:, NBETA * 32:NBETA * 32 + 32], t32c, ALU.mult))
            dve_head(dve, 1, 1, True, True, False)
            with dve.Fori(1, NH // 2) as m:
                dve_head(dve, 2 * m, 0, True, True, True)
                dve_head(dve, 2 * m + 1, 1, True, True, True)
            dve_head(dve, NH, 0, False, True, True)
            dve_head(dve, NH + 1, 1, False, False, True)
            for k in range(KT):
                add_to_x(dve, T_DO + k, k % NB, k)
                if k:
                    norm_lo(dve, 4, k - 1)
            norm_lo(dve, 4, KT - 1)
            dve_tail(dve, 1)


def kernel(x, p, positions, mix_norm, attn_w_qkv, attn_q_gain, attn_k_gain, attn_w_o, dn_w_in, dn_conv, dn_a_log,
           dn_dt_bias, dn_o_gain, dn_w_o, mlp_norm, w_up, w_down, ple_norm, w_ple, w_ple_gate):
    import concourse.bacc as _bacc
    from concourse import mybir as _mybir
    from concourse.bass_utils import run_bass_kernel_spmd as _run

    a = {k: np.asarray(v) for k, v in dict(
        x=x, p=p, positions=positions, mix_norm=mix_norm, w_qkv=attn_w_qkv, qg=attn_q_gain, kg=attn_k_gain,
        w_ao=attn_w_o, w_in=dn_w_in, conv=dn_conv, alog=dn_a_log, dt=dn_dt_bias, og=dn_o_gain, w_do=dn_w_o,
        mlp_norm=mlp_norm, w_up=w_up, w_down=w_down, ple_norm=ple_norm, w_ple=w_ple, w_gate=w_ple_gate).items()}

    def tiles(w):
        return w.reshape(-1, P, w.shape[1]).transpose(1, 0, 2).reshape(P, -1)

    def blocks(w, width):
        return [tiles(w[:, n:n + width]) for n in range(0, w.shape[1], width)]

    def tail(layer):
        up, down = blocks(a["w_up"][layer], 256), []
        for q in range(4):
            down.append(blocks(a["w_down"][layer][q * D:(q + 1) * D], 256))
        mlp = [c for q in range(4) for c in up[4 * q:4 * q + 4] + down[q]]
        return mlp[:31] + [tiles(a["w_ple"][layer])] + mlp[31:] + blocks(a["w_gate"][layer], 256)

    stream = []
    for g, _ in GROUPS:
        for what in (1, 0, 2):
            n = (3 * g + what) * AW
            stream += [tiles(a["w_qkv"][0][r:r + 512, n:n + AW]) for r in (0, 512)]
    stream += blocks(a["w_ao"][0], 512) + tail(0)
    w_in = a["w_in"][0]
    zo = 3 * D + 2 * NH
    for h in range(NH):
        for l, r in ((0, D), (2 * D, zo)):
            stream.append(tiles(np.concatenate([w_in[:, l + h * P:l + (h + 1) * P], w_in[:, r + h * P:r + (h + 1) * P]], axis=1)))
    stream += blocks(a["w_do"][0], 256) + tail(1)

    params = np.zeros((P, N_PARAM), np.float32)

    def put(name, v):
        params[:, _P[name][0]:_P[name][1]] = v

    gains = [a[n][layer].reshape(KT, P).T for layer in range(2) for n in ("mix_norm", "mlp_norm", "ple_norm")]
    put("gain", np.concatenate(gains, axis=1))
    for name in ("qg", "kg"):
        put(name, np.concatenate([a[name][0][g] for g, _ in GROUPS])[None, :])
    put("conv", a["conv"][0].reshape(4, 3, NH, P).transpose(3, 2, 1, 0).reshape(P, NH * 12))
    put("og", a["og"][0][:, None])
    put("dt", a["dt"][0][None, :])
    put("alog", a["alog"][0][None, :])

    t = a["positions"][0]
    pos = np.concatenate([t.reshape(P, TT), t.reshape(TT, P).T], axis=1)

    ins = {
        "xT": a["x"][0].T.reshape(KT, P, S).transpose(1, 0, 2),
        "pT": np.concatenate([tiles(a["p"][layer][0].T) for layer in range(2)], axis=1),
        "pos": pos,
        "weights": np.stack(stream),
        "wab": tiles(w_in[:, 3 * D:zo]),
        "consts": constants(),
        "params": params,
    }
    nc = _bacc.Bacc("TRN2", target_bir_lowering=False, num_devices=1)
    arrays, args = {}, []
    for name, v in ins.items():
        arrays[f"in_{name}"] = np.ascontiguousarray(v)
        args.append(nc.dram_tensor(f"in_{name}", v.shape, _mybir.dt.from_np(v.dtype), kind="ExternalInput").ap())
    scratch = [nc.dram_tensor(f"records{g}", (S, REC), F32, kind="Internal").ap() for g in range(2)]
    out = nc.dram_tensor("out_x", (P, KT, S), F32, kind="ExternalOutput").ap()
    trunk(nc, *args, scratch, out)
    r = _run(nc, [arrays], core_ids=[0])
    return r.results[0]["out_x"].transpose(1, 0, 2).reshape(D, S).T.reshape(1, S, D)
```

```python
from contextlib import ExitStack

import numpy as np
import concourse.bass as bass
from concourse import mybir

F32 = mybir.dt.float32
F32R = mybir.dt.float32r
I32 = mybir.dt.int32
ALU = mybir.AluOpType
ACT = mybir.ActivationFunctionType
AX = mybir.AxisListType.X

P = 128
S = 512
D = 1024
KT = D // P
TT = S // P
CH = 2048
EPS = 1e-6

HD = 64
AH = 8
AW = AH * HD
GROUPS = ((0, 1), (2, 4), (1, 4))
REC = AW + 2 * AH
ASCALE = HD ** -0.5
NEG = -1e30
RD = 16
HR = RD // 2

NH = 8
QS = float(P) ** -0.5
LEVELS = 7

C_AO, C_MLP, C_GATE, C_DN, C_DO = 18, (20, 77), (53, 110), 57, 73
N_CHUNKS = 114
T_AO, T_MLP, T_GATE, T_DO = 72, (80, 168), (152, 240), 160
NB = 4


_C = {}
_at = 0
for _n, _w in (("ident", P), ("incl", P), ("ones", P), ("strict", P), ("band", 2 * P), ("resid", P),
               ("lev", LEVELS * 64), ("freq", HR), ("eps", 1)):
    _C[_n] = (_at, _at + _w)
    _at += _w
N_CONST = _at
_P = {}
_at = 0
for _n, _w in (("gain", 6 * KT), ("qg", 3 * HD), ("kg", 3 * HD), ("conv", NH * 12), ("og", 1),
               ("dt", NH), ("alog", NH)):
    _P[_n] = (_at, _at + _w)
    _at += _w
N_PARAM = _at


def constants():
    i = np.arange(P)
    c = np.zeros((P, N_CONST), np.float32)

    def put(name, v):
        c[:, _C[name][0]:_C[name][1]] = v

    put("ident", np.eye(P))
    put("incl", i[:, None] <= i[None, :])
    put("ones", 1.0)
    put("strict", i[:, None] < i[None, :])
    put("band", np.concatenate([np.where(i[None, :] >= i[:, None], 0.0, NEG),
                                np.where(i[None, :] <= i[:, None], 0.0, NEG)], axis=1))
    same = (i[:, None] % 4) == (i[None, :] % 4)
    put("resid", np.where(same & (i[None, :] <= i[:, None]), 0.0, NEG))
    lev = []
    for n in range(LEVELS):
        b = 1 << n
        even = i[(i // b) % 2 == 0]
        lev.append(((i[:, None] // b) % 2 == 1) & ((i[:, None] // (2 * b)) == (even[None, :] // (2 * b))))
    put("lev", np.concatenate(lev, axis=1))
    put("freq", 500000.0 ** (-np.arange(0, RD, 2) / RD))
    put("eps", EPS)
    return c


class Chain:

    def __init__(self, eng, sem, base=0):
        self.eng, self.sem, self.base, self.n = eng, sem, base, 0

    def __call__(self, ins):
        self.n += 1
        ins.then_inc(self.sem, 1)
        self.eng.wait_ge(self.sem, self.base + self.n)


def rsqrt_guess(dve, link, x, y, t):
    link(dve.tensor_scalar(t.bitcast(I32), x.bitcast(I32), 1, None, ALU.logical_shift_right))
    link(dve.tensor_scalar(y.bitcast(I32), t.bitcast(I32), -1.0, float(0x5F3759DF), ALU.mult, ALU.add))


def rsqrt_step(dve, link, x, y, t, done=None):
    link(dve.tensor_tensor(t, y, y, ALU.mult))
    link(dve.scalar_tensor_tensor(t, t, -0.5, x, ALU.mult, ALU.mult))
    last = dve.scalar_tensor_tensor(y, t, 1.5, y, ALU.add, ALU.mult)
    if done is not None:
        last.then_inc(done, 1)
    else:
        link(last)


def rsqrt(dve, link, x, y, t, done=None):
    rsqrt_guess(dve, link, x, y, t)
    for step in range(3):
        rsqrt_step(dve, link, x, y, t, done if step == 2 else None)


def wait(eng, sem, count):
    if not isinstance(count, int) or count > 0:
        eng.wait_ge(sem, count)



def trunk(nc, xT, pT, pos, weights, wab, consts, params, scratch, out):
    ctx = ExitStack()
    with ctx:
        def sb(name, shape, dt=F32):
            return ctx.enter_context(nc.sbuf_tensor(name, [P] + shape, dt))

        def sem(name):
            return ctx.enter_context(nc.semaphore(name))

        x = sb("x_res", [KT, S])
        A_hi, A_lo = sb("A_hi", [KT, S], F32R), sb("A_lo", [KT, S], F32R)
        B_hi, B_lo = sb("B_hi", [KT, S], F32R), sb("B_lo", [KT, S], F32R)
        raw = sb("raw", [2, CH])
        w_hi, w_lo = sb("w_hi", [2, CH], F32R), sb("w_lo", [2, CH], F32R)
        cst, par = sb("cst", [N_CONST]), sb("par", [N_PARAM])
        work, small = sb("work", [17100]), sb("small", [1000])
        posi, kint = sb("posi", [8], I32), sb("kint", [8 * HR], I32)
        ab_hi, ab_lo = sb("ab_hi", [KT, 16], F32R), sb("ab_lo", [KT, 16], F32R)
        pg = [ctx.enter_context(nc.psum_tensor(f"pg{i}", [P, 512], F32)) for i in range(NB)]
        pa = [ctx.enter_context(nc.psum_tensor(f"pa{i}", [P, 512], F32)) for i in range(4)]

        used = {}

        def carve(pool, n, at=None):
            t = work if pool == "work" else small
            a = used.get(pool, 0) if at is None else at
            used[pool] = a + n
            assert used[pool] <= t.shape[1], (pool, used[pool])
            return t[:, a:a + n]

        def C(name, a=0, b=None):
            lo, hi = _C[name]
            return cst[:, lo + a:(hi if b is None else lo + b)]

        def Pm(name, a=0, b=None):
            lo, hi = _P[name]
            return par[:, lo + a:(hi if b is None else lo + b)]

        ident, ones = C("ident"), C("ones")

        rstd = carve("work", S)
        sq = [carve("work", S) for _ in range(2)]
        acc = carve("work", S)
        sdev = carve("work", S)
        relu = [carve("work", S) for _ in range(2)]
        act2 = [carve("work", S) for _ in range(2)]
        ple = carve("work", KT * S).rearrange("p (k s) -> p k s", k=KT)
        p_raw = carve("work", 2 * S)
        y_k, y_q = carve("work", TT * REC, 0), carve("work", TT * REC)
        qT = carve("work", TT * AW).rearrange("p (a s) -> p a s", a=4)
        kT = carve("work", TT * AW).rearrange("p (a s) -> p a s", a=4)
        V = carve("work", TT * AW).rearrange("p (t c) -> p t c", t=TT)
        og = carve("work", TT * REC).rearrange("p (t c) -> p t c", t=TT)
        s_b, p_b, pt_b = carve("work", 4 * 256), carve("work", 4 * 256), carve("work", 2 * 512)
        ysq = [carve("work", 512) for _ in range(2)]
        rt = carve("work", 512)
        asq, aacc = [s_b[:, 0:512], s_b[:, 512:1024]], p_b[:, 0:512]
        rec = [y.rearrange("p (t c) -> p t c", t=TT) for y in (y_k, y_q)]
        omix = ysq
        stage = carve("work", 3 * S, 4 * S).rearrange("p (n s) -> p n s", n=3)
        pre = carve("work", 3 + S)
        nat = carve("work", 2 * S)
        K_T, Q_T, K_n, V_n, Y_T, ATT, z_s = ([carve("work", S) for _ in range(2)] for _ in range(7))
        zraw, DS, gB, DD, o_t = (carve("work", S) for _ in range(5))
        XBT = carve("work", 2 * S)
        X, BT, nsq = XBT[:, 0:S], XBT[:, S:2 * S], XBT
        XT = nat[:, 0:S]
        U = carve("work", 256)
        state, nR, qsS, vnew, vdec = (carve("work", P) for _ in range(5))
        osq, oT, DI = sq[0], sq[1], acc
        abT = K_T[0]

        rcol, rc_x, rc_t = carve("small", 16), carve("small", 16), carve("small", 16)
        ss, rs_, rs_t, mx = carve("small", 32), carve("small", 32), carve("small", 32), carve("small", 4)
        ang, kf, nang = carve("small", 8 * HR), carve("small", 8 * HR), carve("small", 8 * HR)
        C16 = carve("small", 8 * RD).rearrange("p (t e) -> p t e", t=8)
        S8 = carve("small", 8 * HR).rearrange("p (t e) -> p t e", t=8)
        N8 = carve("small", 8 * HR).rearrange("p (t e) -> p t e", t=8)
        mg, mge, mgn, mgd = carve("small", 96, 148), carve("small", 96), ss, rs_
        dcol = carve("small", 6 * 32, 16 * 3)
        g_c, t32a, t32b, t32c, u32, eb = (carve("small", 32) for _ in range(6))
        mx8 = carve("small", 8)
        hcol = [carve("small", 6 * TT) for _ in range(2)]
        cw = carve("small", 12)
        dss, drs, drt = carve("small", 8), carve("small", 8), carve("small", 8)
        oss, ors, ort = carve("small", 4), carve("small", 4), carve("small", 4)
        GC, NBETA, BETA, EGC, NBKD, CDEC = range(6)

        x_loaded = [sem(f"x_loaded{j}") for j in range(4)]
        par_loaded, c_loaded, pos_loaded, ab_loaded = sem("par_loaded"), sem("c_loaded"), sem("pos_loaded"), sem("ab_loaded")
        p_loaded, out_stored = sem("p_loaded"), sem("out_stored")
        raw_loaded = [sem("raw_loaded0"), sem("raw_loaded1")]
        chunk_hi, chunk_lo = sem("chunk_hi"), sem("chunk_lo")
        tile_done, act_read, dve_read = sem("tile_done"), sem("act_read"), sem("dve_read")
        x_ready, h_hi, h_lo, sq_ready, acc_ready = sem("x_ready"), sem("h_hi"), sem("h_lo"), sem("sq_ready"), sem("acc_ready")
        ssq_full, sd_ready, rstd_ready = sem("ssq_full"), sem("sd_ready"), sem("rstd_ready")
        rcol_full, rcol_ready = sem("rcol_full"), sem("rcol_ready")
        hid_hi, relu2_ready, hid_lo = sem("hid_hi"), sem("relu2_ready"), sem("hid_lo")
        gate_sig, gate_mul = sem("gate_sig"), sem("gate_mul")
        p_hi, p_lo = sem("p_hi"), sem("p_lo")
        dve_step = sem("dve_step")
        trig_arg, trig_done = sem("trig_arg"), sem("trig_done")
        y_raw, ysq_read, y_gained, y_done = sem("y_raw"), sem("ysq_read"), sem("y_gained"), sem("y_done")
        qk_full, qk_placed = sem("qk_full"), sem("qk_placed")
        sc_full, sc_read, max_ready, p_ready = sem("sc_full"), sem("sc_read"), sem("max_ready"), sem("p_ready")
        pt_full, pt_placed, o_full, o_placed = sem("pt_full"), sem("pt_placed"), sem("o_full"), sem("o_placed")
        rec_stored = [sem("rec_stored0"), sem("rec_stored1")]
        rec_loaded = [sem("rec_loaded0"), sem("rec_loaded1")]
        mg_arg, mg_exp, mg_coef = sem("mg_arg"), sem("mg_exp"), sem("mg_coef")
        mg_others, omix_ready = sem("mg_others"), sem("omix_ready")
        mt_full, mt_hi, mt_lo = sem("mt_full"), sem("mt_hi"), sem("mt_lo")

        block = ctx.enter_context(nc.Block())

        def used_up(c):
            if c < C_AO:
                return 4 * (c + 1)
            if c < C_MLP[0]:
                return T_AO + 4 * (c - C_AO + 1)
            for layer in range(2):
                k = c - C_MLP[layer]
                if 0 <= k < 33:
                    return T_MLP[layer] + (2 * (k + 1) if k < 31 else 70 if k == 31 else 72)
                if 0 <= c - C_GATE[layer] < 4:
                    return T_GATE[layer] + 2 * (c - C_GATE[layer] + 1)
            return T_DO + 2 * (c - C_DO + 1)

        def split_hi(act, loads, slot, done=None, count=None):
            act.wait_ge(raw_loaded[slot], 16 * loads)
            if done is not None:
                act.wait_ge(done, count)
            nc.scalar.activation(w_hi[:, slot, :], raw[:, slot, :], ACT.Copy).then_inc(chunk_hi, 1)

        def split_lo(pool, c, slot, ops=nc.gpsimd):
            pool.wait_ge(chunk_hi, c + 1)
            ops.tensor_tensor(w_lo[:, slot, :], raw[:, slot, :], w_hi[:, slot, :].bitcast(F32),
                                    ALU.subtract).then_inc(chunk_lo, 1)

        def split_next(act, c):
            if c + 1 < N_CHUNKS:
                if c == 0:
                    split_hi(act, 1, 1)
                elif c == C_DO:
                    split_hi(act, (c + 1) // 2 + 1, (c + 1) % 2, dn_full, 4 * NH)
                else:
                    split_hi(act, (c + 1) // 2 + 1, (c + 1) % 2, tile_done, used_up(c - 1))

        def products(out_ap, lh, ll, rh, rl, start, stop):
            nc.tensor.matmul(out_ap, lh, rh, start=start, stop=False)
            nc.tensor.matmul(out_ap, lh, rl, start=False, stop=False)
            return nc.tensor.matmul(out_ap, ll, rh, start=False, stop=stop)

        def gemm_tile(pe, slot, n, width, t, bank, ks, hi, lo, k_ready=None):
            if isinstance(t, int) and t < T_AO + NB:
                pe.wait_ge(act_read, 36 - NB + (t - T_AO) + 1)
            else:
                pe.wait_ge(dve_read, t - T_AO - NB + 1)
            for k in range(ks):
                if k_ready is not None:
                    k_ready(k)
                a = k * width + n * P
                mm = products(pg[bank][:, :], w_hi[:, slot, a:a + P], w_lo[:, slot, a:a + P],
                              hi[:, k, :], lo[:, k, :], k == 0, k == ks - 1)
            mm.then_inc(tile_done, 1)

        NORM_BUF = [(A_hi, A_lo), (A_hi, A_lo), (A_hi, A_lo), (B_hi, B_lo), (B_hi, B_lo), (B_hi, B_lo)]
        ROW = {1: 1, 2: 2, 3: 3, 4: 4, 5: 5}

        def norm_sq(n):
            return (asq, aacc) if n == 0 else (sq, acc)

        def norm_act(act, n, k):
            e = n * KT + k + 1
            if n == 0:
                act.wait_ge(x_loaded[k // 2], 16)
            else:
                act.wait_ge(*x_count(n, k))
            nc.scalar.activation(NORM_BUF[n][0][:, k, :], x[:, k, :], ACT.Copy,
                                 scale=Pm("gain", n * KT + k, n * KT + k + 1)).then_inc(h_hi, 1)
            if e > 2:
                act.wait_ge(acc_ready, e - 2)
            nc.scalar.activation(norm_sq(n)[0][k % 2], x[:, k, :], ACT.Square).then_inc(sq_ready, 1)

        def norm_lo(dve, n, k):
            dve.wait_ge(h_hi, n * KT + k + 1)
            hi, lo = NORM_BUF[n]
            nc.vector.scalar_tensor_tensor(lo[:, k, :], x[:, k, :], Pm("gain", n * KT + k, n * KT + k + 1),
                                           hi[:, k, :].bitcast(F32), ALU.mult, ALU.subtract).then_inc(h_lo, 1)
            squares, total = norm_sq(n)
            dve.wait_ge(sq_ready, n * KT + k + 1)
            if k == 0:
                if n in ROW and n > 1:
                    dve.wait_ge(ssq_full, ROW[n] - 1)
                nc.vector.tensor_copy(total, squares[0]).then_inc(acc_ready, 1)
            else:
                dve.wait_ge(acc_ready, n * KT + k)
                nc.vector.tensor_tensor(total, total, squares[k % 2], ALU.add).then_inc(acc_ready, 1)

        def norm_row_pe(pe, n):
            pe.wait_ge(acc_ready, (n + 1) * KT)
            if n == 1:
                pe.wait_ge(mt_lo, TT)
            nc.tensor.matmul(pa[0][:, :], ones, acc, start=True, stop=True).then_inc(ssq_full, 1)

        def norm_row_act(act, n):
            act.wait_ge(ssq_full, ROW[n])
            nc.scalar.activation(sdev, pa[0][:, :], ACT.Sqrt, scale=1.0 / D, bias=C("eps")).then_inc(sd_ready, 1)

        def norm_row_dve(dve, n):
            dve.wait_ge(sd_ready, ROW[n])
            nc.vector.reciprocal(rstd, sdev).then_inc(rstd_ready, 1)
            dve.wait_ge(rstd_ready, ROW[n])

        def tokens(row, d, j):
            return row[:, j:S:d] if d > 1 else row[:, j * P:(j + 1) * P]

        def norm_cols_pe(pe, n, strides):
            pe.wait_ge(acc_ready, (n + 1) * KT)
            for o, d in enumerate(strides):
                for j in range(TT):
                    mm = nc.tensor.matmul(pa[1][:, o * TT + j:o * TT + j + 1], tokens(norm_sq(n)[1], d, j),
                                          ones[:, 0:1], start=True, stop=True)
            mm.then_inc(rcol_full, 1)

        def norm_cols_dve(dve, link, count, nth):
            dve.wait_ge(rcol_full, nth)
            link(nc.vector.tensor_scalar(rc_x[:, 0:count], pa[1][:, 0:count], 1.0 / D, EPS, ALU.mult, ALU.add))
            rsqrt(nc.vector, link, rc_x[:, 0:count], rcol[:, 0:count], rc_t[:, 0:count], rcol_ready)

        UNITS = 2 * TT

        def key_blocks(gi, u):
            return 2 if GROUPS[gi][1] == 1 and u >= 2 else 1

        PT_BEFORE = {}
        total_pt = 0
        for gi in range(3):
            for u in range(UNITS):
                PT_BEFORE[gi, u] = total_pt
                total_pt += key_blocks(gi, u)
            PT_BEFORE[gi, UNITS] = total_pt

        SLOTS = 72
        TAIL = 12
        FIRST = ([24 + 2 * u for u in range(UNITS)], [48 + 8 * u // 5 for u in range(UNITS)], [69 + u for u in range(UNITS)])
        SCHEDULE = {}

        def rides(slot, *what):
            SCHEDULE.setdefault(slot, []).append(what)

        for gi in range(3):
            for tt in range(TT):
                rides(24 * gi + 8 + tt, "finish", gi, tt)
                rides(24 * gi + 16 + tt, "finish", gi, TT + tt)
                rides(24 * gi + (16 + tt, 18 + tt // 2, 15 + tt)[gi], "turn", gi, tt)
                rides(24 * gi + (20, 20, 19)[gi] + tt, "turn", gi, TT + tt)
            for u, at in enumerate(FIRST[gi]):
                rides(at, "scores", gi, u)
                rides(at + 2, "probs", gi, u)
                if key_blocks(gi, u) == 2:
                    rides(at + 3, "probs2", gi, u)
                rides(at + (4 if gi == 0 else 3), "values", gi, u)
        rides(SLOTS + 5, "weigh", 3, 0)
        for tt in range(TT):
            rides(SLOTS + 6 + tt, "merge", 3, tt)
            rides(SLOTS + 7 + tt, "mix", 3, tt)
        ORDER = ("values", "turn", "probs", "probs2", "weigh", "merge", "mix", "scores", "finish")

        def riders(s):
            return sorted(SCHEDULE.get(s, []), key=lambda w: ORDER.index(w[0]))

        def dual(gi, u):
            return (0, 256) if GROUPS[gi][1] == 1 else ((u % 2) * 512, P)

        @block.sync
        def _(sp):
            sp.dma_start(par[:, :], params).then_inc(par_loaded, 16)
            sp.dma_start(raw[:, 0, :], weights[0, :, :]).then_inc(raw_loaded[0], 16)
            sp.dma_start(x[:, 0:2, :], xT[:, 0:2, :]).then_inc(x_loaded[0], 16)
            for j in range(1, 4):
                sp.dma_start(x[:, 2 * j:2 * j + 2, :], xT[:, 2 * j:2 * j + 2, :]).then_inc(x_loaded[j], 16)
            sp.dma_start(raw[:, 1, :], weights[1, :, :]).then_inc(raw_loaded[1], 16)
            sp.dma_start(cst[:, :], consts).then_inc(c_loaded, 16)
            with sp.Fori(1, N_CHUNKS // 2) as m:
                for slot in range(2):
                    sp.wait_ge(chunk_lo, 2 * m + slot - 1)
                    sp.dma_start(raw[:, slot, :], weights[2 * m + slot, :, :]).then_inc(raw_loaded[slot], 16)
            for k in range(KT):
                sp.wait_ge(x_ready, KT + k + 1)
                sp.dma_start(out[:, k, :], x[:, k, :]).then_inc(out_stored, 16)
            sp.wait_ge(out_stored, 16 * KT)

        def x_count(n, k):
            if n in (1, 4):
                return dve_read, (0 if n == 1 else T_DO - T_AO) + k + 1
            if n in (2, 5):
                t = T_MLP[n // 4] + (56 + k if k < 6 else 70 + k - 6)
                return dve_read, t - T_AO + 1
            return x_ready, k + 1

        def pe_quarter(pe, layer, q, first=False, last=False):
            n, c0, t0 = 3 * layer + 1, C_MLP[layer], T_MLP[layer]
            din, hid = ((A_hi, A_lo), (B_hi, B_lo)) if layer == 0 else ((B_hi, B_lo), (A_hi, A_lo))
            for ck in range(4):
                pe.wait_ge(chunk_lo, c0 + 8 * q + ck + 1)
                for j in range(2):
                    gemm_tile(pe, (c0 + ck) % 2, j, 2 * P, t0 + 16 * q + 2 * ck + j, (2 * ck + j) % NB, KT, *din,
                              lambda k: pe.wait_ge(h_lo, n * KT + k + 1) if first and ck == 0 and j == 0 else None)
                    if first and ck == 0 and j == 0:
                        norm_row_pe(pe, n)
            for ck in range(4):
                if last and ck == 3:
                    t = t0 + 62
                    pe.wait_ge(chunk_lo, c0 + 31 + 1)
                    pe.wait_ge(p_lo, layer + 1)
                    for j in range(KT):
                        gemm_tile(pe, (c0 + 31) % 2, j, KT * P, t + j, (t + j) % NB, 2, din[0][:, 6:8, :], din[1][:, 6:8, :])
                c, t = c0 + 4 + ck, t0 + 16 * q + 8 + 2 * ck
                if last and ck == 3:
                    c, t = c0 + 32 - 8 * q, t0 + 70
                pe.wait_ge(chunk_lo, c + 8 * q + 1)
                for j in range(2):
                    gemm_tile(pe, c % 2, j, 2 * P, t + j, ((2 * ck if not (last and ck == 3) else 70) + j) % NB, KT, *hid,
                              lambda k: pe.wait_ge(hid_lo, 32 * layer + 8 * q + k + 1) if ck == 0 and j == 0 else None)

        def pe_tail(pe, layer):
            pe_quarter(pe, layer, 0, first=True)
            with pe.Fori(1, 3) as q:
                pe_quarter(pe, layer, q)
            pe_quarter(pe, layer, 3, last=True)
            n, din = 3 * layer + 2, NORM_BUF[3 * layer + 2]
            for ck in range(4):
                c, t = C_GATE[layer] + ck, T_GATE[layer] + 2 * ck
                pe.wait_ge(chunk_lo, c + 1)
                for j in range(2):
                    gemm_tile(pe, c % 2, j, 2 * P, t + j, (t + j) % NB, KT, *din,
                              lambda k: pe.wait_ge(h_lo, n * KT + k + 1) if ck == 0 and j == 0 else None)
                    if ck == 0 and j == 0:
                        norm_row_pe(pe, n)

        def turn(bank, src):
            for a in range(4):
                mm = nc.tensor.transpose(bank[:, a * P:(a + 1) * P], src[:, a * P:(a + 1) * P], ident)
            return mm

        def pe_attention(pe, kind, gi, u):
            j, half, n = u // 2, u % 2, gi * UNITS + u
            if kind == "turn":
                m = gi * 8 + u
                pe.wait_ge(y_done, m + 1)
                wait(pe, qk_placed, m)
                if gi and u == 0:
                    pe.wait_ge(pt_placed, PT_BEFORE[gi - 1, UNITS])
                turn(pa[2], (y_k, y_q)[u // 4][:, (u % 4) * AW:(u % 4 + 1) * AW]).then_inc(qk_full, 1)
            elif kind == "scores":
                pe.wait_ge(qk_placed, gi * 8 + TT + j + 1)
                wait(pe, sc_read, 2 * n)
                wide = key_blocks(gi, u) == 2
                k0, kw = ((j - 1) * P, 2 * P) if wide else (j * P, P)
                for b in range(2):
                    for a in range(2):
                        rows = slice(b * HD, (b + 1) * HD)
                        mm = nc.tensor.matmul(pa[b][:, a * 256:a * 256 + kw], qT[rows, 2 * half + a, j * P:(j + 1) * P],
                                              kT[rows, 2 * half + a, k0:k0 + kw], start=True, stop=True)
                mm.then_inc(sc_full, 1)
            elif kind in ("probs", "probs2"):
                pe.wait_ge(p_ready, 4 * (n + 1))
                pe.wait_ge(qk_placed, (gi + 1) * 8)
                at, w = dual(gi, u)
                b = int(kind == "probs2")
                wait(pe, pt_placed, PT_BEFORE[gi, u] + b)
                for h in range(4):
                    mm = nc.tensor.transpose(pa[2][:, h * P:(h + 1) * P],
                                             p_b[:, at + h * w + b * P:at + h * w + (b + 1) * P], ident)
                mm.then_inc(pt_full, 1)
            elif kind == "values":
                blocks, at = key_blocks(gi, u), dual(gi, u)[0]
                pe.wait_ge(pt_placed, PT_BEFORE[gi, u] + blocks)
                pe.wait_ge(act_read, (gi * 3 + 2) * TT + j + 1)
                if half == 0:
                    wait(pe, o_placed, gi * TT + j)
                for h in range(4):
                    hh = 4 * half + h
                    for b in range(blocks):
                        mm = nc.tensor.matmul(pa[3][:, hh * HD:(hh + 1) * HD],
                                              pt_b[:, at + b * 512 + h * P:at + b * 512 + (h + 1) * P],
                                              V[:, j - blocks + 1 + b, hh * HD:(hh + 1) * HD],
                                              start=(b == 0), stop=(b == blocks - 1))
                mm.then_inc(o_full, 1)
            elif kind == "mix":
                pe.wait_ge(omix_ready, u + 1)
                turn(pg[u], omix[u % 2]).then_inc(mt_full, 1)

        STEPS = 28
        TILES = [2 if 8 <= s < 12 else 1 for s in range(STEPS)]
        FULL_AT = [next(s for s in range(STEPS) if sum(TILES[:s + 1]) >= KT * (n + 1)) for n in range(4)]
        assert sum(TILES) == 4 * KT

        EARLY = {(NH, 3 + 2 * n): (n % 2, n // 2) for n in range(12)}
        EARLY |= {(NH + 1, 1 + n): (2 + n % 2, n // 2) for n in range(12)}
        EARLY |= {(NH + 1, 13 + n): (n, NH - 2) for n in range(4)}

        def output_product(j, k):
            slot, a = (C_DO + j // 2) % 2, (k * 2 + j % 2) * P
            return products(pg[j][:, :], w_hi[:, slot, a:a + P], w_lo[:, slot, a:a + P], A_hi[:, k, :], A_lo[:, k, :],
                            k == 0, k == NH - 1)

        def pe_gates(pe, s):
            if s == FULL_AT[0]:
                norm_row_pe(pe, 3)
            if s == FULL_AT[0] + 1:
                pe.wait_ge(ab_split, 2)
                for k in range(KT):
                    mm = products(pa[1][0:16, :], ab_hi[:, k, :], ab_lo[:, k, :], B_hi[:, k, :], B_lo[:, k, :], k == 0, k == KT - 1)
                mm.then_inc(abT_full, 1)
            if s == 16:
                pe.wait_ge(abT_ready, 1)
                for tt in range(TT):
                    mm = nc.tensor.transpose(pa[2][:, tt * 16:(tt + 1) * 16], abT[0:16, tt * P:(tt + 1) * P], ident[0:16, 0:16])
                mm.then_inc(ab_full, 1)

        def pe_head(pe, i, par_, g, inv, scan, first=False):
            h, hi_, hs = i, i - 1, i - 2
            PA, PB, pI = pg[2], pg[3], pa[0]
            pv = 1 - par_
            for s in range(STEPS):
                for tile in range(sum(TILES[:s]), sum(TILES[:s + 1])) if g else ():
                    n, k = divmod(tile, KT)
                    if first and n == 0:
                        pe.wait_ge(h_lo, 3 * KT + k + 1)
                    if k == 0:
                        if n % 2 == 0:
                            pe.wait_ge(chunk_lo, C_DN + 2 * h + n // 2 + 1)
                        wait(pe, dn_read, 4 * h + n - 1)
                    a = k * 2 * P + (n % 2) * P
                    sl = (C_DN + n // 2) % 2
                    mm = products(pg[n % 2][:, :], w_hi[:, sl, a:a + P], w_lo[:, sl, a:a + P], B_hi[:, k, :], B_lo[:, k, :],
                                  k == 0, k == KT - 1)
                    if k == KT - 1:
                        mm.then_inc(dn_full, 1)
                if first:
                    pe_gates(pe, s)
                if not g and (i, s) in EARLY:
                    j, k = EARLY[i, s]
                    if k == 0 and j < 2:
                        pe.wait_ge(dn_read, 4 * NH)
                        pe.wait_ge(chunk_lo, C_DO + 1)
                    elif k == 0:
                        pe.wait_ge(XT_placed, LEVELS * NH)
                        pe.wait_ge(att_done, NH)
                        pe.wait_ge(chunk_lo, C_DO + 2)
                    pe.wait_ge(oT_lo, k + 1)
                    output_product(j, k)
                if inv:
                    if s == 0:
                        pe.wait_ge(dn_silu, 4 * hi_ + 2)
                        wait(pe, XT_placed, LEVELS * hi_)
                        wait(pe, att_done, hi_)
                        turn(PA, stage[:, 0, :]).then_inc(tq_full, 1)
                        turn(PB, stage[:, 1, :]).then_inc(tk_full, 1)
                    if s == 2:
                        pe.wait_ge(dn_silu, 4 * hi_ + 3)
                        pe.wait_ge(nq_placed, hi_ + 1)
                        turn(PA, stage[:, 2, :]).then_inc(tv_full, 1)
                    if s == 3:
                        pe.wait_ge(nk_placed, hi_ + 1)
                        pe.wait_ge(gB_ready, hi_ + 1)
                        for t in range(TT):
                            mm = nc.tensor.matmul(PB[:, t * P:(t + 1) * P], gB[:, t * P:(t + 1) * P], C("incl"), start=True, stop=True)
                        mm.then_inc(gcb_full, 1)
                    if s == 9:
                        pe.wait_ge(v_placed, hi_ + 1)
                        pe.wait_ge(kn_ready, hi_ + 1)
                        turn(PA, K_n[pv]).then_inc(tkn_full, 1)
                    if s == 10:
                        pe.wait_ge(dd_ready, hi_ + 1)
                        pe.wait_ge(qn_ready, hi_ + 1)
                        turn(PB, nat[:, 0:S]).then_inc(tqn_full, 1)
                    if s == 11:
                        pe.wait_ge(KT_placed, hi_ + 1)
                        for t in range(TT):
                            b = slice(t * P, (t + 1) * P)
                            mm = nc.tensor.matmul(PA[:, b], K_T[pv][:, b], K_T[pv][:, b], start=True, stop=True)
                        mm.then_inc(G_full, 1)
                    if s == 12:
                        pe.wait_ge(QT_placed, hi_ + 1)
                        for t in range(TT):
                            b = slice(t * P, (t + 1) * P)
                            mm = nc.tensor.matmul(PB[:, b], K_T[pv][:, b], Q_T[pv][:, b], start=True, stop=True)
                        mm.then_inc(QK_full, 1)
                    for what, l in inverse_steps(s):
                        bs = 1 << l
                        if what == "U":
                            if l == 0:
                                pe.wait_ge(BT_ready, hi_ + 1)
                            wait(pe, X_done, LEVELS * hi_ + l)
                            for t in range(TT):
                                src = ident if l == 0 else X[:, t * P:(t + 1) * P]
                                mm = nc.tensor.matmul(pI[:, t * 64:(t + 1) * 64], BT[:, t * P:(t + 1) * P], even(src, bs),
                                                      start=True, stop=True)
                            mm.then_inc(U_full, 1)
                        elif what == "XU":
                            pe.wait_ge(U_placed, LEVELS * hi_ + l + 1)
                            pe.wait_ge(XT_placed, LEVELS * hi_ + l)
                            for t in range(TT):
                                mm = nc.tensor.matmul(pI[:, 256 + t * 64:256 + (t + 1) * 64], XT[:, t * P:(t + 1) * P],
                                                      U[:, t * 64:(t + 1) * 64], start=True, stop=True)
                            mm.then_inc(XU_full, 1)
                        else:
                            pe.wait_ge(X_done, LEVELS * hi_ + l + 1)
                            wait(pe, XT_placed, LEVELS * hi_ + l)
                            turn(PA, X).then_inc(XT_full, 1)
                if scan:
                    tt, st = divmod(s - 1, 6)
                    b = slice(tt * P, (tt + 1) * P)
                    if s >= 1 and tt < TT and st == 0:
                        if tt == 0:
                            pe.wait_ge(XT_placed, LEVELS * (hs + 1))
                        pe.wait_ge(state_ready, 4 * hs + tt + 1)
                        nc.tensor.matmul(pa[1][:, 0:P], K_T[par_][:, b], state, start=True, stop=True).then_inc(KS_full, 1)
                        wait(pe, qs_ready, 4 * hs + tt)
                        if tt == 0:
                            wait(pe, oT_ready, hs)
                        nc.tensor.matmul(pa[3][:, 0:P], Q_T[par_][:, b], state, start=True, stop=True).then_inc(QS_full, 1)
                    if s >= 1 and tt < TT and st == 2:
                        pe.wait_ge(nR_ready, 4 * hs + tt + 1)
                        wait(pe, o_done, 4 * hs + tt)
                        nc.tensor.matmul(pa[2][:, 0:P], Y_T[par_][:, b], nR, start=True, stop=True).then_inc(YR_full, 1)
                    if s >= 1 and tt < TT and st == 4:
                        pe.wait_ge(vn_ready, 4 * hs + tt + 1)
                        nc.tensor.matmul(pa[2][:, P:2 * P], ATT[par_][:, b], vnew, start=True, stop=True).then_inc(O_full, 1)
                        if tt < TT - 1:
                            pe.wait_ge(vd_ready, 3 * hs + tt + 1)
                            nc.tensor.matmul(pa[1][:, P:2 * P], K_n[par_][:, b], vdec, start=True, stop=True).then_inc(SN_full, 1)
                    if s == 26:
                        pe.wait_ge(on_ready, hs + 1)
                        pe.wait_ge(qs_ready, 4 * hs + 4)
                        turn(pa[3], o_t).then_inc(oT_full, 1)

        (dn_full, dn_read, dn_silu, dn_tap, dn_conv, tq_full, tk_full, tv_full, gcb_full, tkn_full, tqn_full,
         G_full, QK_full, nq_placed, nk_placed, v_placed, KT_placed, QT_placed, gB_ready, dd_ready, D_ready, DS_ready,
         DI_ready, nsq_ready, kn_ready, qn_ready, BT_ready, att_done, X_init, X_done, U_full, U_placed,
         XU_full, XT_full, XT_placed, KS_full, QS_full, YR_full, O_full, SN_full, nR_ready, qs_ready, vn_ready,
         vd_ready, o_done, state_ready, osq_ready, on_ready, oT_full, oT_ready, oT_hi, oT_lo) = (
            sem(n) for n in """dn_full dn_read dn_silu dn_tap dn_conv tq_full tk_full tv_full gcb_full
            tkn_full tqn_full G_full QK_full nq_placed nk_placed v_placed KT_placed QT_placed gB_ready dd_ready D_ready
            DS_ready DI_ready nsq_ready kn_ready qn_ready BT_ready att_done X_init X_done U_full U_placed
            XU_full XT_full XT_placed KS_full QS_full YR_full O_full SN_full nR_ready qs_ready vn_ready vd_ready o_done
            state_ready osq_ready on_ready oT_full oT_ready oT_hi oT_lo""".split())
        ab_split, ab_full, g_arg, g_exp, g_ready, gc_full, gc_ready, g_cols = (
            sem(n) for n in "ab_split ab_full g_arg g_exp g_ready gc_full gc_ready g_cols".split())
        gemm_link, inv_link, scan_link, gate_link = sem("gemm_link"), sem("inv_link"), sem("scan_link"), sem("gate_link")
        abT_full, abT_ready = sem("abT_full"), sem("abT_ready")
        GEMM_LINKS, INV_LINKS, SCAN_LINKS = 7, 14, 12

        def even(m, b):
            return m.rearrange("p (a two b) -> p a two b", two=2, b=b)[:, :, 0, :]

        INV = [[("U", 0)], [("T", 0), ("U", 1)]]
        for _l in range(1, LEVELS):
            INV.append([("XU", _l)])
            INV.append([("T", _l)] + ([("U", _l + 1)] if _l + 1 < LEVELS else []))
        INV_SLOT = [13 + j for j in range(len(INV))]

        def inverse_steps(s):
            return [x_ for j, st in enumerate(INV) if INV_SLOT[j] == s for x_ in st]

        @block.tensor
        def _(pe):
            for s in range(SLOTS + TAIL):
                if s < SLOTS:
                    sec, half, tt = s // 8, (s // 4) % 2, s % 4
                    c, d = 2 * sec + half, GROUPS[sec // 3][1]
                    if s == 4:
                        pe.wait_ge(c_loaded, 16)
                        norm_cols_pe(pe, 0, (4, 1))
                    if tt == 0:
                        pe.wait_ge(chunk_lo, c + 1)
                    if half == 0:
                        wait(pe, act_read, (sec - 1) * TT + tt + 1)
                    for kk in range(4):
                        k = half * 4 + kk
                        if s in (0, 4):
                            pe.wait_ge(h_lo, k + 1)
                        mm = products(pg[tt][:, :], tokens(A_hi[:, k, :], d, tt), tokens(A_lo[:, k, :], d, tt),
                                      w_hi[:, c % 2, kk * 512:(kk + 1) * 512], w_lo[:, c % 2, kk * 512:(kk + 1) * 512],
                                      k == 0, k == KT - 1)
                    mm.then_inc(tile_done, 1)
                for kind, gi, u in riders(s):
                    pe_attention(pe, kind, gi, u)
            for ck in range(2):
                pe.wait_ge(chunk_lo, C_AO + ck + 1)
                if ck == 0:
                    pe.wait_ge(mt_lo, TT)
                for j in range(4):
                    t = T_AO + 4 * ck + j
                    gemm_tile(pe, ck, j, 4 * P, t, t % NB, 4, B_hi, B_lo)
            pe_tail(pe, 0)
            pe.wait_ge(dve_read, T_DO - T_AO)
            pe_head(pe, 0, 0, True, False, False, first=True)
            pe.wait_ge(g_ready, 1)
            pe.wait_ge(g_arg, 1)
            nc.tensor.matmul(pa[2][:, 64:96], C("incl"), g_c, start=True, stop=True)
            nc.tensor.matmul(pa[2][:, 96:128], ones, g_c, start=True, stop=True).then_inc(gc_full, 1)
            pe_head(pe, 1, 1, True, True, False)
            pe_head(pe, 2, 0, True, True, True)
            pe_head(pe, 3, 1, True, True, True)
            with pe.Fori(2, NH // 2) as m:
                pe_head(pe, 2 * m, 0, True, True, True)
                pe_head(pe, 2 * m + 1, 1, True, True, True)
            pe_head(pe, NH, 0, False, True, True)
            pe_head(pe, NH + 1, 1, False, False, True)
            pe.wait_ge(oT_lo, NH)
            for j in range(4):
                output_product(j, NH - 1).then_inc(tile_done, 1)
            for ck in range(2, 4):
                c, t = C_DO + ck, T_DO + 2 * ck
                pe.wait_ge(chunk_lo, c + 1)
                for j in range(2):
                    gemm_tile(pe, c % 2, j, 2 * P, t + j, (t + j) % NB, KT, A_hi, A_lo)
            pe_tail(pe, 1)

        def act_quarter(act, layer, q, last=False):
            n, c0, t0 = 3 * layer + 1, C_MLP[layer], T_MLP[layer]
            din, hid = (A_hi, B_hi) if layer == 0 else (B_hi, A_hi)
            for ck in range(4):
                k = 8 * q + ck
                split_hi(act, (c0 + ck + 1) // 2 + 1 + 4 * q, (c0 + ck + 1) % 2, tile_done, t0 + 2 * k)
                for j in range(2):
                    act.wait_ge(dve_read, t0 + 16 * q + 2 * ck + j - T_AO + 1)
                    nc.scalar.activation(hid[:, 2 * ck + j, :], relu[j], ACT.Square).then_inc(hid_hi, 1)
            if last:
                act.wait_ge(p_loaded, 16 * (layer + 1))
                act.wait_ge(tile_done, t0 + 56)
                nc.scalar.activation(din[:, 6:8, :], p_raw, ACT.Copy).then_inc(p_hi, 1)
            for ck in range(4):
                if last:
                    for cc in ([c0 + 28 + ck] if ck < 3 else [c0 + 31, c0 + 32]):
                        split_next(act, cc)
                    for j in range(2):
                        norm_act(act, n + 1, 2 * ck + j)
                else:
                    k = 8 * q + 4 + ck
                    split_hi(act, (c0 + 4 + ck + 1) // 2 + 1 + 4 * q, (c0 + ck + 1) % 2, tile_done, t0 + 2 * k)

        def act_tail(act, layer):
            n = 3 * layer + 1
            act.wait_ge(dve_read, (0, T_DO - T_AO)[layer] + KT)
            act.dma_start(p_raw, pT[:, layer * 1024:(layer + 1) * 1024]).then_inc(p_loaded, 16)
            norm_row_act(act, n)
            act_quarter(act, layer, 0)
            with act.Fori(1, 3) as q:
                act_quarter(act, layer, q)
            act_quarter(act, layer, 3, last=True)
            norm_row_act(act, n + 1)
            for ck in range(4):
                split_next(act, C_GATE[layer] + ck)
                for j in range(2):
                    k = 2 * ck + j
                    act.wait_ge(dve_read, T_GATE[layer] - T_AO + k + 1)
                    wait(act, x_ready, 8 * layer + k - 1)
                    nc.scalar.activation(act2[j], relu[j], ACT.Sigmoid).then_inc(gate_sig, 1)
                    if layer == 0 and k:
                        norm_act(act, 3, k - 1)
            if layer == 0:
                norm_act(act, 3, KT - 1)

        def act_attention(act, kind, gi, u):
            j, half, n = u // 2, u % 2, gi * UNITS + u
            if kind == "scores":
                kw = key_blocks(gi, u) * P
                at, w = dual(gi, u)
                act.wait_ge(max_ready, n + 1)
                wait(act, pt_full, PT_BEFORE[gi, max(0, u - (w == P))])
                for h in range(4):
                    hh = 4 * half + h
                    o = at + h * w
                    nc.scalar.activation(p_b[:, o:o + kw], s_b[:, o:o + kw], ACT.Exp,
                                         bias=og[:, j, AW + hh:AW + hh + 1], scale=ASCALE,
                                         accum_out=og[:, j, AW + AH + hh:AW + AH + hh + 1]).then_inc(p_ready, 1)
            elif kind == "values" and half == 1:
                act.wait_ge(o_full, n + 1)
                nc.scalar.activation(og[:, j, 0:AW], pa[3][:, :], ACT.Copy).then_inc(o_placed, 1)
                if gi < 2 and u == UNITS - 1:
                    act.wait_ge(o_placed, (gi + 1) * TT)
                    act.wait_ge(p_ready, 4 * (gi + 1) * UNITS)
                    act.dma_start(scratch[gi].rearrange("(t p) c -> p t c", p=P), og).then_inc(rec_stored[gi], 16)
            elif kind == "weigh":
                act.wait_ge(mg_arg, 1)
                nc.scalar.activation(mge, mg, ACT.Exp).then_inc(mg_exp, 1)
            elif kind == "mix":
                act.wait_ge(mt_full, u + 1)
                nc.scalar.activation(B_hi[:, 0:4, u:S:TT], pg[u][:, :].rearrange("p (a t) -> p a t", a=4),
                                     ACT.Copy).then_inc(mt_hi, 1)

        def act_gates(act, s):
            if s == FULL_AT[0] - 1:
                norm_row_act(act, 3)
            if s == 16:
                act.wait_ge(g_arg, 1)
                nc.scalar.activation(t32c, t32b, ACT.Exp).then_inc(g_exp, 1)
                nc.scalar.activation(mx8, Pm("alog"), ACT.Exp).then_inc(g_exp, 1)
                nc.scalar.activation(eb, t32a, ACT.Exp).then_inc(g_exp, 1)
                act.wait_ge(g_exp, 3)
                nc.scalar.activation(t32c, t32c, ACT.Ln, bias=1.0).then_inc(g_exp, 1)

        def act_head(act, i, par_, g, inv, scan, first=False):
            h, hi_, hs = i, i - 1, i - 2
            PA, PB = pg[2], pg[3]
            pv = 1 - par_
            for s in range(STEPS):
                if g and s == 0:
                    if isinstance(h, int) and h == 0:
                        split_hi(act, 30, 0, tile_done, T_DO)
                    else:
                        split_hi(act, 30 + h, 0, dn_full, 4 * h)
                if g and s == 14:
                    split_hi(act, 30 + h, 1, dn_full, 4 * h + 2)
                if first:
                    act_gates(act, s)
                if inv:
                    if s == 0:
                        act.wait_ge(tq_full, hi_ + 1)
                        nc.scalar.activation(nat[:, 0:S], PA[:, :], ACT.Copy).then_inc(nq_placed, 1)
                        act.wait_ge(tk_full, hi_ + 1)
                        nc.scalar.activation(nat[:, S:2 * S], PB[:, :], ACT.Copy).then_inc(nk_placed, 1)
                    if s in (2, 4):
                        act.wait_ge(nq_placed if s == 2 else nk_placed, hi_ + 1)
                        if s == 2:
                            wait(act, X_done, LEVELS * hi_)
                            wait(act, qn_ready, hi_)
                        for t in range(TT) if s == 2 else range(TT, 2 * TT):
                            b = slice(t * P, (t + 1) * P)
                            ins = nc.scalar.activation(nsq[:, b], nat[:, b], ACT.Square, accum_out=dss[:, t:t + 1])
                        ins.then_inc(nsq_ready, 1)
                    if s == 3:
                        act.wait_ge(tv_full, hi_ + 1)
                        nc.scalar.activation(V_n[pv], PA[:, :], ACT.Copy).then_inc(v_placed, 1)
                    if s == 5:
                        act.wait_ge(dd_ready, hi_ + 1)
                        nc.scalar.activation(DD, DD, ACT.Exp).then_inc(D_ready, 1)
                    if s == 9:
                        act.wait_ge(tkn_full, hi_ + 1)
                        nc.scalar.activation(K_T[pv], PA[:, :], ACT.Copy).then_inc(KT_placed, 1)
                    if s == 10:
                        act.wait_ge(tqn_full, hi_ + 1)
                        nc.scalar.activation(Q_T[pv], PB[:, :], ACT.Copy).then_inc(QT_placed, 1)
                    for what, l in inverse_steps(s):
                        if what == "T":
                            act.wait_ge(XT_full, LEVELS * hi_ + l + 1)
                            nc.scalar.activation(Y_T[pv] if l == LEVELS - 1 else XT, PA[:, :], ACT.Copy).then_inc(XT_placed, 1)
                if scan:
                    tt, st = divmod(s - 1, 6)
                    if s >= 1 and tt < TT and st == 0:
                        act.wait_ge(QS_full, 4 * hs + tt + 1)
                        wait(act, o_done, 4 * hs + tt)
                        nc.scalar.activation(qsS, pa[3][:, 0:P], ACT.Copy,
                                             scale=hcol[par_][:, EGC * TT + tt:EGC * TT + tt + 1]).then_inc(qs_ready, 1)
                    if s >= 1 and tt < TT and st == 5:
                        act.wait_ge(o_done, 4 * hs + tt + 1)
                        if tt == 0:
                            wait(act, on_ready, hs)
                        b = slice(tt * P, (tt + 1) * P)
                        nc.scalar.activation(osq[:, b], o_t[:, b], ACT.Square, accum_out=oss[:, tt:tt + 1]).then_inc(osq_ready, 1)
                    if s == STEPS - 1:
                        act.wait_ge(oT_ready, hs + 1)
                        nc.scalar.activation(A_hi[:, hs, :], oT, ACT.Copy).then_inc(oT_hi, 1)
                if g and s in FULL_AT[:3]:
                    n = FULL_AT.index(s)
                    act.wait_ge(dn_read, 4 * h + n + 1)
                    if n == 0:
                        wait(act, tq_full, h)
                    elif n == 1:
                        wait(act, tk_full, h)
                    else:
                        wait(act, tv_full, h)
                    nc.scalar.activation(stage[:, n, :], pre[:, 3:3 + S], ACT.Copy,
                                         scale=cw[:, 4 * n + 3:4 * n + 4]).then_inc(dn_tap, 1)
                if g and s - 4 in FULL_AT[:3]:
                    n = FULL_AT.index(s - 4)
                    act.wait_ge(dn_conv, 3 * h + n + 1)
                    nc.scalar.activation(stage[:, n, :], stage[:, n, :], ACT.Silu).then_inc(dn_silu, 1)
                if g and s == STEPS - 1:
                    act.wait_ge(dn_read, 4 * h + 4)
                    nc.scalar.activation(z_s[par_], zraw, ACT.Silu).then_inc(dn_silu, 1)

        @block.scalar
        def _(act):
            act.dma_start(posi[:, :], pos).then_inc(pos_loaded, 16)
            act.dma_start(rt[:, 0:KT * 16], wab).then_inc(ab_loaded, 16)
            act.wait_ge(par_loaded, 16)
            for k in range(KT):
                if k == 0:
                    split_hi(act, 1, 0)
                norm_act(act, 0, k)
            split_next(act, 0)
            act.wait_ge(ab_loaded, 16)
            nc.scalar.activation(ab_hi[:, :, :], rt[:, 0:KT * 16].rearrange("p (k c) -> p k c", c=16), ACT.Copy).then_inc(ab_split, 1)
            act.wait_ge(trig_arg, 2)
            nc.scalar.activation(S8[:, :, :], ang.rearrange("p (t e) -> p t e", t=8), ACT.Sin).then_inc(trig_done, 1)
            nc.scalar.activation(C16[:, :, 0:HR], nang.rearrange("p (t e) -> p t e", t=8), ACT.Sin).then_inc(trig_done, 1)
            for s in range(SLOTS + TAIL):
                if s < SLOTS:
                    sec, half, tt = s // 8, (s // 4) % 2, s % 4
                    if tt == 0 and s:
                        split_next(act, 2 * sec + half)
                    if half == 1:
                        gi, what = divmod(sec, 3)
                        r0 = rcol[:, (TT if GROUPS[gi][1] == 1 else 0) + tt:][:, 0:1]
                        act.wait_ge(tile_done, 4 * (2 * sec + 1) + tt + 1)
                        if s < 8:
                            act.wait_ge(rcol_ready, 1)
                        if what == 2:
                            if gi and tt == 0:
                                act.wait_ge(o_full, gi * UNITS)
                            nc.scalar.activation(V[:, tt, :], pg[tt][:, :], ACT.Copy, scale=r0).then_inc(act_read, 1)
                        else:
                            n = (gi * 2 + what) * TT + tt
                            if gi:
                                act.wait_ge(qk_full, (gi - 1) * 8 + 4 * (what + 1))
                            nc.scalar.activation((y_k, y_q)[what][:, tt * AW:(tt + 1) * AW], pg[tt][:, :], ACT.Copy,
                                                 scale=r0).then_inc(y_raw, 1)
                            wait(act, ysq_read, n - 1)
                            nc.scalar.activation(ysq[tt % 2], pg[tt][:, :], ACT.Square, scale=r0).then_inc(act_read, 1)
                for kind, gi, u in riders(s):
                    act_attention(act, kind, gi, u)
                if s == SLOTS - 1:
                    for g_, order in enumerate(("(p t) c -> p t c", "(t p) c -> p t c")):
                        act.wait_ge(rec_stored[g_], 16)
                        act.wait_ge(qk_full, 16 + 4 * (g_ + 1))
                        act.dma_start(rec[g_], scratch[g_].rearrange(order, p=P)).then_inc(rec_loaded[g_], 16)
            for ck in range(2):
                split_next(act, C_AO + ck)
                for j in range(4):
                    norm_act(act, 1, 4 * ck + j)
            act_tail(act, 0)
            act_head(act, 0, 0, True, False, False, first=True)
            act.wait_ge(gc_ready, 1)
            nc.scalar.activation(dcol[:, EGC * 32:EGC * 32 + 32], dcol[:, GC * 32:GC * 32 + 32], ACT.Exp).then_inc(g_cols, 1)
            nc.scalar.activation(t32c, t32b, ACT.Exp).then_inc(g_cols, 1)
            nc.scalar.activation(dcol[:, CDEC * 32:CDEC * 32 + 32], t32a, ACT.Exp).then_inc(g_cols, 1)
            act_head(act, 1, 1, True, True, False)
            act_head(act, 2, 0, True, True, True)
            act_head(act, 3, 1, True, True, True)
            with act.Fori(2, NH // 2) as m:
                act_head(act, 2 * m, 0, True, True, True)
                act_head(act, 2 * m + 1, 1, True, True, True)
            split_next(act, C_DO)
            act_head(act, NH, 0, False, True, True)
            act_head(act, NH + 1, 1, False, False, True)
            for ck in range(4):
                if ck:
                    split_next(act, C_DO + ck)
                for j in range(2):
                    norm_act(act, 4, 2 * ck + j)
            act_tail(act, 1)

        def coef(g_, u):
            return mge[:, (g_ * TT + u) * AH:(g_ * TT + u + 1) * AH]

        def heads_view(t):
            return t.rearrange("p (h e) -> p h e", e=HD)

        def per_head(col, heads=AH):
            return col.unsqueeze(2).to_broadcast([P, heads, HD])

        def pool_quarter(pool, layer, q, last=False):
            c0, t0 = C_MLP[layer], T_MLP[layer]
            for ck in range(4):
                split_lo(pool, c0 + 8 * q + ck + 1, (c0 + ck + 1) % 2)
                for j in range(2):
                    e = 32 * layer + 8 * q + 2 * ck + j + 1
                    pool.wait_ge(dve_read, t0 + 16 * q + 2 * ck + j - T_AO + 1)
                    wait(pool, hid_lo, e - 2)
                    nc.gpsimd.tensor_tensor(act2[j], relu[j], relu[j], ALU.mult).then_inc(relu2_ready, 1)
            for ck in range(4):
                if last:
                    for cc in ([c0 + 28 + ck] if ck < 3 else [c0 + 31, c0 + 32]):
                        split_lo(pool, cc + 1, (cc + 1) % 2)
                else:
                    split_lo(pool, c0 + 8 * q + 4 + ck + 1, (c0 + ck + 1) % 2)

        def pool_tail(pool, layer):
            pool_quarter(pool, layer, 0)
            with pool.Fori(1, 3) as q:
                pool_quarter(pool, layer, q)
            pool_quarter(pool, layer, 3, last=True)
            for ck in range(4):
                c = C_GATE[layer] + ck
                if c + 1 < N_CHUNKS:
                    split_lo(pool, c + 1, (c + 1) % 2)

        def pool_head(pool, i, par_, g, inv, scan):
            h, hi_, hs = i, i - 1, i - 2
            for s in range(STEPS):
                if g and s == 0:
                    split_lo(pool, C_DN + 2 * h + 1, 0)
                if g and s == 14:
                    split_lo(pool, C_DN + 2 * h + 2, 1)
                if inv:
                    if s == 6:
                        pool.wait_ge(D_ready, hi_ + 1)
                        wait(pool, att_done, hi_)
                        nc.gpsimd.tensor_tensor(bank4(DS), bank4(DD), four(C("strict")), ALU.mult).then_inc(DS_ready, 1)
                        nc.gpsimd.tensor_tensor(bank4(DI), bank4(DD), four(C("incl")), ALU.mult).then_inc(DI_ready, 1)
                    if s == 7:
                        pool.wait_ge(nsq_ready, 2 * hi_ + 2)
                        nc.gpsimd.tensor_tensor(bank4(X), four(ident), four(ident), ALU.mult).then_inc(X_init, 1)

        def bank4(t):
            return t.rearrange("p (t c) -> p t c", t=TT)

        def four(m, n=TT):
            return m.unsqueeze(1).to_broadcast([P, n, m.shape[1]])

        @block.gpsimd
        def _(pool):
            pool.wait_ge(chunk_lo, 1)
            for s in range(SLOTS + TAIL):
                if s < SLOTS:
                    sec, half, tt = s // 8, (s // 4) % 2, s % 4
                    if tt == 0:
                        split_lo(pool, 2 * sec + half + 1, (half + 1) % 2)
                    gi, what = divmod(sec, 3)
                    if half == 1 and what < 2:
                        n = (gi * 2 + what) * TT + tt
                        pool.wait_ge(y_raw, n + 1)
                        y = heads_view((y_k, y_q)[what][:, tt * AW:(tt + 1) * AW])
                        gain = Pm("kg" if what == 0 else "qg", gi * HD, (gi + 1) * HD)
                        nc.gpsimd.tensor_tensor(y, y, four(gain, AH), ALU.mult).then_inc(y_gained, 1)
                for kind, _g, u in riders(s):
                    if kind == "merge":
                        pool.wait_ge(rec_loaded[0], 16)
                        pool.wait_ge(rec_loaded[1], 16)
                        pool.wait_ge(mg_coef, 1)
                        for g_ in range(2):
                            o_ = heads_view(rec[g_][:, u, 0:AW])
                            nc.gpsimd.tensor_tensor(o_, o_, per_head(coef(g_, u)), ALU.mult).then_inc(mg_others, 1)
            for ck in range(2):
                split_lo(pool, C_AO + ck + 1, (C_AO + ck + 1) % 2)
            pool_tail(pool, 0)
            pool_head(pool, 0, 0, True, False, False)
            pool_head(pool, 1, 1, True, True, False)
            pool_head(pool, 2, 0, True, True, True)
            pool_head(pool, 3, 1, True, True, True)
            with pool.Fori(2, NH // 2) as m:
                pool_head(pool, 2 * m, 0, True, True, True)
                pool_head(pool, 2 * m + 1, 1, True, True, True)
            split_lo(pool, C_DO + 1, (C_DO + 1) % 2)
            pool_head(pool, NH, 0, False, True, True)
            pool_head(pool, NH + 1, 1, False, False, True)
            pool.wait_ge(chunk_lo, C_DO + 4)
            split_lo(pool, C_DO + 4, (C_DO + 4) % 2)
            pool_tail(pool, 1)

        def add_to_x(dve, t, bank, k):
            dve.wait_ge(tile_done, t + 1)
            nc.vector.tensor_tensor(x[:, k, :], x[:, k, :], pg[bank][:, :], ALU.add).then_inc(dve_read, 1)
            dve.wait_ge(dve_read, t - T_AO + 1)

        def dve_quarter(dve, layer, q, first=False, last=False):
            n, t0 = 3 * layer + 1, T_MLP[layer]
            hid = (B_hi, B_lo) if layer == 0 else (A_hi, A_lo)
            din = (A_hi, A_lo) if layer == 0 else (B_hi, B_lo)
            if first:
                norm_row_dve(dve, n)

            def low(k):
                e = 32 * layer + 8 * q + k + 1
                dve.wait_ge(hid_hi, e)
                dve.wait_ge(relu2_ready, e)
                nc.vector.tensor_tensor(hid[1][:, k, :], act2[k % 2], hid[0][:, k, :].bitcast(F32), ALU.subtract).then_inc(hid_lo, 1)

            for k in range(8):
                t = t0 + 16 * q + k
                e = 32 * layer + 8 * q + k + 1
                dve.wait_ge(tile_done, t + 1)
                wait(dve, hid_hi, e - 2)
                wait(dve, relu2_ready, e - 2)
                nc.vector.scalar_tensor_tensor(relu[k % 2], pg[k % NB][:, :], 0.0, rstd, ALU.max, ALU.mult).then_inc(dve_read, 1)
                if k:
                    low(k - 1)
            low(7)
            for k in range(8):
                t, bank = t0 + 16 * q + 8 + k, k % NB
                if last and k == 0:
                    dve.wait_ge(p_hi, layer + 1)
                    nc.vector.tensor_tensor(din[1][:, 6:8, :], p_raw, din[0][:, 6:8, :].bitcast(F32), ALU.subtract).then_inc(p_lo, 1)
                if last and k == 6:
                    for j in range(KT):
                        dve.wait_ge(tile_done, t0 + 62 + j + 1)
                        nc.vector.tensor_copy(ple[:, j, :], pg[(62 + j) % NB][:, :]).then_inc(dve_read, 1)
                if last and k >= 6:
                    t, bank = t0 + 70 + k - 6, (70 + k - 6) % NB
                add_to_x(dve, t, bank, k)
                if last and k:
                    norm_lo(dve, n + 1, k - 1)
            if last:
                norm_lo(dve, n + 1, 7)

        def dve_tail(dve, layer):
            dve_quarter(dve, layer, 0, first=True)
            with dve.Fori(1, 3) as q:
                dve_quarter(dve, layer, q)
            dve_quarter(dve, layer, 3, last=True)
            norm_row_dve(dve, 3 * layer + 2)

            def gated(k):
                dve.wait_ge(gate_sig, 8 * layer + k + 1)
                nc.vector.tensor_tensor(act2[k % 2], act2[k % 2], ple[:, k, :], ALU.mult).then_inc(gate_mul, 1)
                dve.wait_ge(gate_mul, 8 * layer + k + 1)
                nc.vector.tensor_tensor(x[:, k, :], x[:, k, :], act2[k % 2], ALU.add).then_inc(x_ready, 1)

            for k in range(KT):
                t = T_GATE[layer] + k
                dve.wait_ge(tile_done, t + 1)
                wait(dve, gate_sig, 8 * layer + k - 1)
                nc.vector.tensor_tensor(relu[k % 2], pg[k % NB][:, :], rstd, ALU.mult).then_inc(dve_read, 1)
                if k:
                    gated(k - 1)
                if layer == 0 and k > 1:
                    norm_lo(dve, 3, k - 2)
            gated(KT - 1)
            if layer == 0:
                norm_lo(dve, 3, KT - 2)
                norm_lo(dve, 3, KT - 1)

        def dve_attention(dve, link, kind, gi, u):
            j, half, n = u // 2, u % 2, gi * UNITS + u
            if kind == "finish":
                finish_y(dve, link, gi, u // TT, u % TT)
            elif kind == "turn":
                m = gi * 8 + u
                tt = u % 4
                dve.wait_ge(qk_full, m + 1)
                if gi and u % 4 == 0:
                    dve.wait_ge(sc_full, gi * UNITS)
                nc.vector.tensor_copy((kT, qT)[u // 4][:, :, tt * P:(tt + 1) * P],
                                      pa[2][:, :].rearrange("p (a t) -> p a t", a=4)).then_inc(qk_placed, 1)
            elif kind == "scores":
                wide = key_blocks(gi, u) == 2
                kw = 2 * P if wide else P
                at, w = dual(gi, u)
                mask = C("resid") if GROUPS[gi][0] == 2 else C("band", 0 if wide else P)
                dve.wait_ge(sc_full, n + 1)
                wait(dve, p_ready, 4 * (n - (w == P and u > 0)))
                mine = s_b[:, at:at + 4 * w]
                s4 = mine.rearrange("p (a b c) -> p b a c", a=2, b=2)
                for b in range(2):
                    nc.vector.tensor_tensor(s4[:, b, :, 0:kw], pa[b][:, :].rearrange("p (a c) -> p a c", a=2)[:, :, 0:kw],
                                            four(mask, 2), ALU.add).then_inc(sc_read, 1)
                dve.wait_ge(sc_read, 2 * n + 2)
                link(nc.vector.tensor_reduce(mx, mine.rearrange("p (h c) -> p h c", h=4)[:, :, 0:kw], AX, ALU.max))
                if n == gi * UNITS and gi:
                    dve.wait_ge(rec_stored[gi - 1], 16)
                nc.vector.tensor_scalar(og[:, j, AW + 4 * half:AW + 4 * half + 4], mx, -ASCALE, None, ALU.mult).then_inc(max_ready, 1)
            elif kind in ("probs", "probs2"):
                at, w = dual(gi, u)
                b = int(kind == "probs2")
                dve.wait_ge(pt_full, PT_BEFORE[gi, u] + b + 1)
                wait(dve, o_full, n - (w == P and u > 0))
                nc.vector.tensor_copy(pt_b[:, at + b * 512:at + (b + 1) * 512], pa[2][:, :]).then_inc(pt_placed, 1)
            elif kind == "weigh":
                dve.wait_ge(rec_loaded[0], 16)
                dve.wait_ge(rec_loaded[1], 16)
                dve.wait_ge(p_ready, 4 * 3 * UNITS)
                recs = [rec[0], rec[1], og]
                nm = [r[:, :, AW:AW + AH] for r in recs]
                den = [r[:, :, AW + AH:REC] for r in recs]
                mg4 = mg.rearrange("p (g t h) -> p g t h", g=3, t=TT)
                mge4 = mge.rearrange("p (g t h) -> p g t h", g=3, t=TT)
                mgn3, mgd3 = (m_.rearrange("p (t h) -> p t h", t=TT) for m_ in (mgn, mgd))
                link(nc.vector.tensor_tensor(mgn3, nm[0], nm[1], ALU.min))
                link(nc.vector.tensor_tensor(mgn3, mgn3, nm[2], ALU.min))
                for g_ in range(3):
                    ins = nc.vector.tensor_tensor(mg4[:, g_], mgn3, nm[g_], ALU.subtract)
                ins.then_inc(mg_arg, 1)
                dve.wait_ge(mg_exp, 1)
                for g_ in range(3):
                    ins = nc.vector.tensor_tensor(mg4[:, g_], mge4[:, g_], den[g_], ALU.mult)
                link(ins)
                link(nc.vector.tensor_tensor(mgd3, mg4[:, 0], mg4[:, 1], ALU.add))
                link(nc.vector.tensor_tensor(mgd3, mgd3, mg4[:, 2], ALU.add))
                link(nc.vector.reciprocal(mgd, mgd))
                nc.vector.tensor_tensor(mge.rearrange("p (g n) -> p g n", g=3), mge.rearrange("p (g n) -> p g n", g=3),
                                        mgd.unsqueeze(1).to_broadcast([P, 3, TT * AH]), ALU.mult).then_inc(mg_coef, 1)
                dve.wait_ge(mg_coef, 1)
            elif kind == "merge":
                dve.wait_ge(o_placed, 2 * TT + u + 1)
                wait(dve, mt_full, u - 1)
                o_ = omix[u % 2]
                link(nc.vector.tensor_tensor(heads_view(o_), heads_view(og[:, u, 0:AW]), per_head(coef(2, u)), ALU.mult))
                dve.wait_ge(mg_others, 2 * u + 2)
                link(nc.vector.tensor_tensor(o_, o_, rec[0][:, u, 0:AW], ALU.add))
                nc.vector.tensor_tensor(o_, o_, rec[1][:, u, 0:AW], ALU.add).then_inc(omix_ready, 1)
            elif kind == "mix":
                dve.wait_ge(mt_hi, u + 1)
                b = slice(u, S, TT)
                nc.vector.tensor_tensor(B_lo[:, 0:4, b], pg[u][:, :].rearrange("p (a t) -> p a t", a=4),
                                        B_hi[:, 0:4, b].bitcast(F32), ALU.subtract).then_inc(mt_lo, 1)

        def finish_y(dve, link, gi, what, tt):
            n = gi * 2 + what
            y = (y_k, y_q)[what][:, tt * AW:(tt + 1) * AW]
            if tt == 0:
                link(nc.vector.tensor_scalar(ss, ss, 1.0 / HD, EPS, ALU.mult, ALU.add))
                rsqrt(nc.vector, link, ss, rs_, rs_t)
            dve.wait_ge(y_gained, n * TT + tt + 1)
            link(nc.vector.tensor_tensor(heads_view(y), heads_view(y), per_head(rs_[:, tt * AH:(tt + 1) * AH]), ALU.mult))
            y3 = heads_view(y)
            r3 = rt[:, 0:AH * RD].rearrange("p (h e) -> p h e", e=RD)
            o = (TT if GROUPS[gi][1] == 1 else 0) + tt

            def table(tab, w):
                return tab[:, o:o + 1, :].to_broadcast([P, AH, w])

            nc.vector.tensor_tensor(r3[:, :, 0:HR], y3[:, :, HR:RD], table(N8, HR), ALU.mult)
            link(nc.vector.tensor_tensor(r3[:, :, HR:RD], y3[:, :, 0:HR], table(S8, HR), ALU.mult))
            link(nc.vector.tensor_tensor(y3[:, :, 0:RD], y3[:, :, 0:RD], table(C16, RD), ALU.mult))
            nc.vector.tensor_tensor(y3[:, :, 0:RD], y3[:, :, 0:RD], r3, ALU.add).then_inc(y_done, 1)
            dve.wait_ge(y_done, n * TT + tt + 1)

        def rope_tables(dve, link):
            dve.wait_ge(pos_loaded, 16)
            link(nc.vector.tensor_copy(rc_t[:, 0:8], posi[:, :]))
            a3 = ang.rearrange("p (t e) -> p t e", t=8)
            link(nc.vector.tensor_tensor(a3, rc_t[:, 0:8].unsqueeze(2).to_broadcast([P, 8, HR]), four(C("freq"), 8), ALU.mult))
            link(nc.vector.tensor_scalar(kint[:, :], ang, 1.0 / (2 * np.pi), None, ALU.mult))
            link(nc.vector.tensor_copy(kf, kint[:, :]))
            c1 = 6.28125
            c2 = float(np.round((2 * np.pi - c1) * 2**20) / 2**20)
            c3 = float(np.float32(2 * np.pi - c1 - c2))
            for part in (c1, c2, c3):
                link(nc.vector.scalar_tensor_tensor(ang, kf, -part, ang, ALU.mult, ALU.add))
            lim = 3.1415925
            link(nc.vector.tensor_scalar(ang, ang, -lim, lim, ALU.max, ALU.min))
            nc.vector.tensor_scalar(kf, ang, -1.0, None, ALU.mult).then_inc(trig_arg, 1)
            dve.wait_ge(trig_arg, 1)
            link(nc.vector.tensor_tensor(kf, kf, ang, ALU.max))
            nc.vector.tensor_scalar(nang, kf, -1.0, float(np.pi / 2), ALU.mult, ALU.add).then_inc(trig_arg, 1)
            dve.wait_ge(trig_done, 2)
            link(nc.vector.tensor_scalar(N8[:, :, :], S8[:, :, :], -1.0, None, ALU.mult))
            link(nc.vector.tensor_copy(C16[:, :, HR:RD], C16[:, :, 0:HR]))

        def dve_gates(dve, link, s):
            if s == FULL_AT[0]:
                norm_row_dve(dve, 3)
            if s == FULL_AT[0] + 1:
                dve.wait_ge(abT_full, 1)
                nc.vector.tensor_tensor(abT[0:16, :], pa[1][0:16, :], rstd[0:16, :], ALU.mult).then_inc(abT_ready, 1)
            if s == 16:
                dve.wait_ge(ab_full, 1)
                ab4 = pa[2][:, 0:64].rearrange("p (t c) -> p t c", t=TT)
                v4 = lambda t: t.rearrange("p (t h) -> p t h", t=TT)
                link(nc.vector.tensor_tensor(v4(u32), ab4[:, :, 0:NH], four(Pm("dt")), ALU.add))
                link(nc.vector.scalar_tensor_tensor(t32b, u32, -1.0, u32, ALU.mult, ALU.min))
                nc.vector.tensor_scalar(v4(t32a), ab4[:, :, NH:2 * NH], -87.0, -1.0, ALU.max, ALU.mult).then_inc(g_arg, 1)
            if s == 20:
                dve.wait_ge(g_exp, 4)
                link(nc.vector.scalar_tensor_tensor(u32, u32, 0.0, t32c, ALU.max, ALU.add))
                v4 = lambda t: t.rearrange("p (t h) -> p t h", t=TT)
                nc.vector.scalar_tensor_tensor(v4(g_c), v4(u32), -1.0, four(mx8), ALU.mult, ALU.mult).then_inc(g_ready, 1)
                link(nc.vector.tensor_scalar(eb, eb, 1.0, None, ALU.add))
                link(nc.vector.reciprocal(dcol[:, BETA * 32:BETA * 32 + 32], eb))
                link(nc.vector.tensor_scalar(dcol[:, NBETA * 32:NBETA * 32 + 32], dcol[:, BETA * 32:BETA * 32 + 32], -1.0, None, ALU.mult))

        def dve_head(dve, i, par_, g, inv, scan, first=False):
            h, hi_, hs = i, i - 1, i - 2
            pv = 1 - par_
            PA, PB, pI = pg[2], pg[3], pa[0]
            glink = Chain(dve, gemm_link, h * GEMM_LINKS)
            ilink = Chain(dve, inv_link, hi_ * INV_LINKS)
            slink = Chain(dve, scan_link, hs * SCAN_LINKS)

            def col(p_, q, t):
                return hcol[p_][:, q * TT + t:q * TT + t + 1]

            for s in range(STEPS):
                if g and s == 0:
                    wait(dve, dn_conv, 3 * h)
                    glink(nc.vector.tensor_copy(cw, Pm("conv").rearrange("p (h c) -> p h c", c=12)[:, h, :]))
                if inv and s == 0:
                    wait(dve, o_done, 4 * hs)
                    ilink(nc.vector.tensor_copy(hcol[pv], dcol.rearrange("p (q h) -> p q h", h=NH)[:, :, hi_]))
                    nc.vector.tensor_copy(bank4(gB), g_c.rearrange("p (t h) -> p t h", h=NH)[:, :, hi_].unsqueeze(2)
                                          .to_broadcast([P, TT, P])).then_inc(gB_ready, 1)
                if inv and s == 25:
                    nc.vector.memset(state, 0.0).then_inc(state_ready, 1)
                    dve.wait_ge(state_ready, 4 * hi_ + 1)
                if inv:
                    for what, l in inverse_steps(s):
                        bs = 1 << l
                        if what == "U":
                            dve.wait_ge(U_full, LEVELS * hi_ + l + 1)
                            nc.vector.tensor_tensor(U.rearrange("p (t c) -> p t c", t=TT), pI[:, 0:256].rearrange("p (t c) -> p t c", t=TT),
                                                    four(C("lev", l * 64, (l + 1) * 64)), ALU.mult).then_inc(U_placed, 1)
                            dve.wait_ge(U_placed, LEVELS * hi_ + l + 1)
                        if (what, l) == ("U", 0):
                            dve.wait_ge(X_init, hi_ + 1)
                            ev = even(X, bs)
                            nc.vector.tensor_tensor(ev, ev, U.rearrange("p (a b) -> p a b", b=bs), ALU.subtract).then_inc(X_done, 1)
                            dve.wait_ge(X_done, LEVELS * hi_ + 1)
                        if what == "XU":
                            dve.wait_ge(XU_full, (LEVELS - 1) * hi_ + l)
                            ev = even(X, bs)
                            nc.vector.tensor_tensor(ev, ev, pI[:, 256:512].rearrange("p (a b) -> p a b", b=bs), ALU.subtract).then_inc(X_done, 1)
                            dve.wait_ge(X_done, LEVELS * hi_ + l + 1)
                if scan:
                    tt, st = divmod(s - 1, 6)
                    if s >= 1 and tt < TT:
                        b = slice(tt * P, (tt + 1) * P)
                        e = 4 * hs + tt + 1
                        if st == 0:
                            dve.wait_ge(KS_full, e)
                            nc.vector.scalar_tensor_tensor(nR, pa[1][:, 0:P], col(par_, EGC, tt), V_n[par_][:, b],
                                                           ALU.mult, ALU.subtract).then_inc(nR_ready, 1)
                        if st == 2:
                            dve.wait_ge(YR_full, e)
                            wait(dve, O_full, e - 1)
                            if tt < TT - 1:
                                nc.vector.tensor_scalar(vdec, pa[2][:, 0:P], col(par_, NBKD, tt), None, ALU.mult).then_inc(vd_ready, 1)
                            nc.vector.tensor_scalar(vnew, pa[2][:, 0:P], col(par_, NBETA, tt), None, ALU.mult).then_inc(vn_ready, 1)
                        if st == 4:
                            dve.wait_ge(O_full, e)
                            dve.wait_ge(qs_ready, e)
                            if tt == 0:
                                wait(dve, oT_full, hs)
                            nc.vector.tensor_tensor(o_t[:, b], pa[2][:, P:2 * P], qsS, ALU.add).then_inc(o_done, 1)
                            if tt < TT - 1:
                                dve.wait_ge(SN_full, 3 * hs + tt + 1)
                                nc.vector.scalar_tensor_tensor(state, state, col(par_, CDEC, tt), pa[1][:, P:2 * P],
                                                               ALU.mult, ALU.add).then_inc(state_ready, 1)
                                dve.wait_ge(state_ready, 4 * hs + tt + 2)
                    if s == 27:
                        dve.wait_ge(oT_full, hs + 1)
                        wait(dve, oT_hi, hs)
                        wait(dve, oT_lo, hs)
                        nc.vector.scalar_tensor_tensor(oT, pa[3][:, :], Pm("og"), z_s[par_], ALU.mult, ALU.mult).then_inc(oT_ready, 1)
                if inv:
                    if s == 4:
                        dve.wait_ge(gcb_full, hi_ + 1)
                        wait(dve, DI_ready, hi_)
                        for t in range(TT):
                            b = slice(t * P, (t + 1) * P)
                            ins = nc.vector.tensor_scalar(DD[:, b], PB[:, b], col(pv, GC, t), 0.0, ALU.subtract, ALU.min)
                        ins.then_inc(dd_ready, 1)
                    if s == 5:
                        dve.wait_ge(nsq_ready, 2 * hi_ + 2)
                        ilink(nc.vector.tensor_scalar(dss, dss, EPS, None, ALU.add))
                        rsqrt_guess(nc.vector, ilink, dss, drs, drt)
                    if s in (6, 7):
                        rsqrt_step(nc.vector, ilink, dss, drs, drt)
                    if s == 8:
                        rsqrt_step(nc.vector, ilink, dss, drs, drt)
                        nc.vector.tensor_tensor(bank4(K_n[pv]), bank4(nat[:, S:2 * S]), drs[:, TT:2 * TT].unsqueeze(2)
                                                .to_broadcast([P, TT, P]), ALU.mult).then_inc(kn_ready, 1)
                    if s == 9:
                        ilink(nc.vector.tensor_scalar(drs[:, 0:TT], drs[:, 0:TT], QS, None, ALU.mult))
                        nc.vector.tensor_tensor(bank4(nat[:, 0:S]), bank4(nat[:, 0:S]), drs[:, 0:TT].unsqueeze(2)
                                                .to_broadcast([P, TT, P]), ALU.mult).then_inc(qn_ready, 1)
                    if s == 12:
                        dve.wait_ge(G_full, hi_ + 1)
                        dve.wait_ge(DS_ready, hi_ + 1)
                        for t in range(TT):
                            b = slice(t * P, (t + 1) * P)
                            ins = nc.vector.scalar_tensor_tensor(BT[:, b], PA[:, b], col(pv, BETA, t), DS[:, b], ALU.mult, ALU.mult)
                        ins.then_inc(BT_ready, 1)
                    if s == 13:
                        dve.wait_ge(QK_full, hi_ + 1)
                        dve.wait_ge(DI_ready, hi_ + 1)
                        nc.vector.tensor_tensor(ATT[pv], PB[:, :], DI, ALU.mult).then_inc(att_done, 1)
                if scan:
                    if s == 24:
                        dve.wait_ge(osq_ready, 4 * hs + 4)
                        slink(nc.vector.tensor_scalar(oss, oss, 1.0 / P, EPS, ALU.mult, ALU.add))
                        rsqrt_guess(nc.vector, slink, oss, ors, ort)
                        rsqrt_step(nc.vector, slink, oss, ors, ort)
                    if s == 25:
                        rsqrt_step(nc.vector, slink, oss, ors, ort)
                        rsqrt_step(nc.vector, slink, oss, ors, ort)
                        nc.vector.tensor_tensor(bank4(o_t), bank4(o_t), ors.unsqueeze(2).to_broadcast([P, TT, P]), ALU.mult).then_inc(on_ready, 1)
                if first:
                    dve_gates(dve, Chain(dve, gate_link, {20: 2}.get(s, 0)), s)
                if g and s in FULL_AT:
                    n = FULL_AT.index(s)
                    dve.wait_ge(dn_full, 4 * h + n + 1)
                    if n < 3:
                        wait(dve, dn_tap, 3 * h + n)
                        wait(dve, dn_conv, 3 * h + n)
                        nc.vector.tensor_tensor(pre[:, 3:3 + S], pg[n % 2][:, :], rstd, ALU.mult).then_inc(dn_read, 1)
                        dve.wait_ge(dn_read, 4 * h + n + 1)
                    else:
                        wait(dve, dn_silu, 4 * h)
                        nc.vector.tensor_tensor(zraw, pg[n % 2][:, :], rstd, ALU.mult).then_inc(dn_read, 1)
                for n, tap in ([(n, n_ + 3 - s) for n, n_ in enumerate(FULL_AT[:3]) if 0 < s - n_ <= 3] if g else ()):
                    if tap == 2:
                        dve.wait_ge(dn_tap, 3 * h + n + 1)
                    ins = nc.vector.scalar_tensor_tensor(stage[:, n, :], pre[:, tap:tap + S], cw[:, 4 * n + tap:4 * n + tap + 1],
                                                         stage[:, n, :], ALU.mult, ALU.add)
                    glink(ins) if tap else ins.then_inc(dn_conv, 1)
                if scan and s == STEPS - 1:
                    dve.wait_ge(oT_hi, hs + 1)
                    nc.vector.tensor_tensor(A_lo[:, hs, :], oT, A_hi[:, hs, :].bitcast(F32), ALU.subtract).then_inc(oT_lo, 1)
            assert not g or glink.n == GEMM_LINKS, glink.n
            assert not inv or ilink.n == INV_LINKS, ilink.n
            assert not scan or slink.n == SCAN_LINKS, slink.n

        @block.vector
        def _(dve):
            link = Chain(dve, dve_step)
            split_lo(dve, 0, 0, nc.vector)
            for k in range(KT):
                norm_lo(dve, 0, k)
            dve.wait_ge(c_loaded, 16)
            norm_cols_dve(dve, link, 8, 1)
            dve.wait_ge(ab_split, 1)
            nc.vector.tensor_tensor(ab_lo[:, :, :], rt[:, 0:KT * 16].rearrange("p (k c) -> p k c", c=16), ab_hi[:, :, :].bitcast(F32),
                                    ALU.subtract).then_inc(ab_split, 1)
            dve.wait_ge(ab_split, 2)
            rope_tables(dve, link)
            for s in range(SLOTS + TAIL):
                for kind, gi, u in riders(s):
                    dve_attention(dve, link, kind, gi, u)
                if s < SLOTS:
                    sec, half, tt = s // 8, (s // 4) % 2, s % 4
                    gi, what = divmod(sec, 3)
                    if half == 1 and what < 2:
                        n = (gi * 2 + what) * TT + tt
                        dve.wait_ge(act_read, sec * TT + tt + 1)
                        nc.vector.tensor_reduce(ss[:, tt * AH:(tt + 1) * AH], heads_view(ysq[tt % 2]), AX, ALU.add).then_inc(ysq_read, 1)
                        dve.wait_ge(ysq_read, n + 1)
            for k in range(KT):
                add_to_x(dve, T_AO + k, k % NB, k)
                if k:
                    norm_lo(dve, 1, k - 1)
            norm_lo(dve, 1, KT - 1)
            dve_tail(dve, 0)
            link(nc.vector.memset(pre[:, 0:3], 0.0))
            dve_head(dve, 0, 0, True, False, False, first=True)
            dve.wait_ge(gc_full, 1)
            link(nc.vector.tensor_copy(dcol[:, GC * 32:GC * 32 + 32], pa[2][:, 64:96]))
            link(nc.vector.tensor_copy(t32a, pa[2][:, 96:128]))
            nc.vector.tensor_tensor(t32b, t32a, dcol[:, GC * 32:GC * 32 + 32], ALU.subtract).then_inc(gc_ready, 1)
            dve.wait_ge(g_cols, 3)
            link(nc.vector.tensor_tensor(dcol[:, NBKD * 32:NBKD * 32 + 32], dcol[:, NBETA * 32:NBETA * 32 + 32], t32c, ALU.mult))
            dve_head(dve, 1, 1, True, True, False)
            dve_head(dve, 2, 0, True, True, True)
            dve_head(dve, 3, 1, True, True, True)
            with dve.Fori(2, NH // 2) as m:
                dve_head(dve, 2 * m, 0, True, True, True)
                dve_head(dve, 2 * m + 1, 1, True, True, True)
            dve_head(dve, NH, 0, False, True, True)
            dve_head(dve, NH + 1, 1, False, False, True)
            for k in range(KT):
                add_to_x(dve, T_DO + k, k % NB, k)
                if k:
                    norm_lo(dve, 4, k - 1)
                if k in (1, 3):
                    split_lo(dve, C_DO + 2 + k // 2, (C_DO + k // 2) % 2, nc.vector)
            norm_lo(dve, 4, KT - 1)
            dve_tail(dve, 1)


def kernel(x, p, positions, mix_norm, attn_w_qkv, attn_q_gain, attn_k_gain, attn_w_o, dn_w_in, dn_conv, dn_a_log,
           dn_dt_bias, dn_o_gain, dn_w_o, mlp_norm, w_up, w_down, ple_norm, w_ple, w_ple_gate):
    import concourse.bacc as _bacc
    from concourse import mybir as _mybir
    from concourse.bass_utils import run_bass_kernel_spmd as _run

    a = {k: np.asarray(v) for k, v in dict(
        x=x, p=p, positions=positions, mix_norm=mix_norm, w_qkv=attn_w_qkv, qg=attn_q_gain, kg=attn_k_gain,
        w_ao=attn_w_o, w_in=dn_w_in, conv=dn_conv, alog=dn_a_log, dt=dn_dt_bias, og=dn_o_gain, w_do=dn_w_o,
        mlp_norm=mlp_norm, w_up=w_up, w_down=w_down, ple_norm=ple_norm, w_ple=w_ple, w_gate=w_ple_gate).items()}

    def tiles(w):
        return w.reshape(-1, P, w.shape[1]).transpose(1, 0, 2).reshape(P, -1)

    def blocks(w, width):
        return [tiles(w[:, n:n + width]) for n in range(0, w.shape[1], width)]

    def tail(layer):
        up, down = blocks(a["w_up"][layer], 256), []
        for q in range(4):
            down.append(blocks(a["w_down"][layer][q * D:(q + 1) * D], 256))
        mlp = [c for q in range(4) for c in up[4 * q:4 * q + 4] + down[q]]
        return mlp[:31] + [tiles(a["w_ple"][layer])] + mlp[31:] + blocks(a["w_gate"][layer], 256)

    stream = []
    for g, _ in GROUPS:
        for what in (1, 0, 2):
            n = (3 * g + what) * AW
            stream += [tiles(a["w_qkv"][0][r:r + 512, n:n + AW]) for r in (0, 512)]
    stream += blocks(a["w_ao"][0], 512) + tail(0)
    w_in = a["w_in"][0]
    zo = 3 * D + 2 * NH
    for h in range(NH):
        for l, r in ((0, D), (2 * D, zo)):
            stream.append(tiles(np.concatenate([w_in[:, l + h * P:l + (h + 1) * P], w_in[:, r + h * P:r + (h + 1) * P]], axis=1)))
    stream += blocks(a["w_do"][0], 256) + tail(1)

    params = np.zeros((P, N_PARAM), np.float32)

    def put(name, v):
        params[:, _P[name][0]:_P[name][1]] = v

    gains = [a[n][layer].reshape(KT, P).T for layer in range(2) for n in ("mix_norm", "mlp_norm", "ple_norm")]
    put("gain", np.concatenate(gains, axis=1))
    for name in ("qg", "kg"):
        put(name, np.concatenate([a[name][0][g] for g, _ in GROUPS])[None, :])
    put("conv", a["conv"][0].reshape(4, 3, NH, P).transpose(3, 2, 1, 0).reshape(P, NH * 12))
    put("og", a["og"][0][:, None])
    put("dt", a["dt"][0][None, :])
    put("alog", a["alog"][0][None, :])

    t = a["positions"][0]
    pos = np.concatenate([t.reshape(P, TT), t.reshape(TT, P).T], axis=1)

    ins = {
        "xT": a["x"][0].T.reshape(KT, P, S).transpose(1, 0, 2),
        "pT": np.concatenate([tiles(a["p"][layer][0].T) for layer in range(2)], axis=1),
        "pos": pos,
        "weights": np.stack(stream),
        "wab": tiles(w_in[:, 3 * D:zo]),
        "consts": constants(),
        "params": params,
    }
    nc = _bacc.Bacc("TRN2", target_bir_lowering=False, num_devices=1)
    arrays, args = {}, []
    for name, v in ins.items():
        arrays[f"in_{name}"] = np.ascontiguousarray(v)
        args.append(nc.dram_tensor(f"in_{name}", v.shape, _mybir.dt.from_np(v.dtype), kind="ExternalInput").ap())
    scratch = [nc.dram_tensor(f"records{g}", (S, REC), F32, kind="Internal").ap() for g in range(2)]
    out = nc.dram_tensor("out_x", (P, KT, S), F32, kind="ExternalOutput").ap()
    trunk(nc, *args, scratch, out)
    r = _run(nc, [arrays], core_ids=[0])
    return r.results[0]["out_x"].transpose(1, 0, 2).reshape(D, S).T.reshape(1, S, D)
```
